# Optimizing a Trainium2 kernel written in Bass

```python
import jax, jax.numpy as jnp
from jax import lax
import numpy as np
import math

D_MODEL = 1024
BATCH = 1
SEQ = 256
DEPTH = 2

PLE_DIM = 256
D_FF = 2752
M_HEADS = 4
M_HEAD_DIM = 256
M_WIDTH = M_HEADS * M_HEAD_DIM
M_CHUNK = 64
CONV_K = 4
A_Q_HEADS = 16
A_KV_HEADS = 4
A_HEAD_DIM = 64
A_GROUP = A_Q_HEADS // A_KV_HEADS
A_WIDTH = A_Q_HEADS * A_HEAD_DIM
A_KV_WIDTH = A_KV_HEADS * A_HEAD_DIM
WINDOW = 128
A_BLOCK = 128
EPS = 1e-6
N_IN = 4 * M_WIDTH + 2 * M_HEADS + A_WIDTH + 2 * A_KV_WIDTH + 2 * D_MODEL


def rmsnorm(x, g):
    xf = x.astype(jnp.float32)
    y = xf * lax.rsqrt(jnp.mean(xf * xf, axis=-1, keepdims=True) + EPS)
    return (y * g.astype(jnp.float32)).astype(x.dtype)

def head_rmsnorm(x, g):
    xf = x.astype(jnp.float32)
    y = xf * lax.rsqrt(jnp.mean(xf * xf, axis=-1, keepdims=True) + EPS)
    return y * g.astype(jnp.float32)

def swiglu(x, w_gate, w_up, w_down):
    return (jax.nn.silu(x @ w_gate) * (x @ w_up)) @ w_down

def causal_dwconv(x, w, b):
    c = x.shape[-1]
    y = lax.conv_general_dilated(x, w[:, None, :].astype(x.dtype), window_strides=(1,),
                                 padding=[(CONV_K - 1, 0)],
                                 dimension_numbers=("NWC", "WIO", "NWC"),
                                 feature_group_count=c)
    return y + b

def mlstm_chunkwise(q, k, v, ig, lf):
    bsz, t, nh, dh = q.shape
    nc = t // M_CHUNK

    def to_chunks(z):
        return z.reshape(bsz, nc, M_CHUNK, nh, dh).transpose(1, 0, 3, 2, 4)

    def g_chunks(z):
        return z.reshape(bsz, nc, M_CHUNK, nh).transpose(1, 0, 3, 2)

    causal = jnp.tril(jnp.ones((M_CHUNK, M_CHUNK), dtype=bool))

    def step(carry, xs):
        c_st, n_st, m_st = carry
        qc, kc, vc, ic, fc = xs
        b = jnp.cumsum(fc, axis=-1)
        dlog = jnp.where(causal, b[..., :, None] - b[..., None, :] + ic[..., None, :], -jnp.inf)
        inter = b + m_st[..., None]
        m_t = jnp.maximum(inter, jnp.max(dlog, axis=-1))
        w_intra = jnp.exp(dlog - m_t[..., None])
        w_inter = jnp.exp(inter - m_t)
        s = jnp.einsum("bhtk,bhsk->bhts", qc, kc) * w_intra
        num = jnp.einsum("bhts,bhsv->bhtv", s, vc) + w_inter[..., None] * jnp.einsum("bhtk,bhvk->bhtv", qc, c_st)
        den = jnp.sum(s, axis=-1) + w_inter * jnp.einsum("bhtk,bhk->bht", qc, n_st)
        h = num / jnp.maximum(jnp.abs(den), jnp.exp(-m_t))[..., None]
        b_last = b[..., -1]
        a = b_last[..., None] - b + ic
        m_new = jnp.maximum(b_last + m_st, jnp.max(a, axis=-1))
        w_state = jnp.exp(a - m_new[..., None])
        decay = jnp.exp(b_last + m_st - m_new)
        c_new = decay[..., None, None] * c_st + jnp.einsum("bhsv,bhsk->bhvk", vc * w_state[..., None], kc)
        n_new = decay[..., None] * n_st + jnp.einsum("bhs,bhsk->bhk", w_state, kc)
        return (c_new, n_new, m_new), h

    init = (jnp.zeros((bsz, nh, dh, dh), jnp.float32),
            jnp.zeros((bsz, nh, dh), jnp.float32),
            jnp.zeros((bsz, nh), jnp.float32))
    xs = (to_chunks(q), to_chunks(k), to_chunks(v), g_chunks(ig), g_chunks(lf))
    _, hs = lax.scan(step, init, xs)
    return hs.transpose(1, 0, 3, 2, 4).reshape(bsz, t, nh, dh)

def swa_gqa_sinks(q, k, v, sinks):
    bsz, t = q.shape[0], q.shape[1]
    nb = t // A_BLOCK
    qb = q.reshape(bsz, nb, A_BLOCK, A_KV_HEADS, A_GROUP, A_HEAD_DIM)

    def windows(z):
        zp = jnp.pad(z, ((0, 0), (A_BLOCK, 0), (0, 0), (0, 0)))
        zb = zp.reshape(bsz, nb + 1, A_BLOCK, A_KV_HEADS, A_HEAD_DIM)
        return jnp.concatenate([zb[:, :-1], zb[:, 1:]], axis=2)

    kw, vw = windows(k), windows(v)
    scores = jnp.einsum("bnqhgd,bnkhd->bnhgqk", qb, kw).astype(jnp.float32) * (A_HEAD_DIM ** -0.5)
    qi = jnp.arange(A_BLOCK)[:, None]
    kj = jnp.arange(2 * A_BLOCK)[None, :]
    rel = A_BLOCK + qi - kj
    band = (rel >= 0) & (rel < WINDOW)
    key_pos = jnp.arange(nb)[:, None, None] * A_BLOCK + kj[None] - A_BLOCK
    valid = band[None] & (key_pos >= 0)
    scores = jnp.where(valid[None, :, None, None], scores, -jnp.inf)
    sink = sinks.astype(jnp.float32).reshape(A_KV_HEADS, A_GROUP)[None, None, :, :, None, None]
    mx = jnp.maximum(jnp.max(scores, axis=-1, keepdims=True), sink)
    pr = jnp.exp(scores - mx)
    den = jnp.sum(pr, axis=-1, keepdims=True) + jnp.exp(sink - mx)
    attn = (pr / den).astype(v.dtype)
    out = jnp.einsum("bnhgqk,bnkhd->bnqhgd", attn, vw)
    return out.reshape(bsz, t, A_WIDTH)

def hybrid_layer(h, p_i, ffn1_norm, ffn1_w_gate, ffn1_w_up, ffn1_w_down, mix_norm, w_in,
                 m_conv_w, m_conv_b, m_igate_b, m_fgate_b, m_out_norm, a_q_norm, a_k_norm,
                 a_sinks, w_branch_m, w_branch_a, w_out, ffn2_norm, ffn2_w_gate, ffn2_w_up,
                 ffn2_w_down, ple_norm, ple_gate_w, ple_proj_w):
    bsz, t, _ = h.shape
    h = h + 0.5 * swiglu(rmsnorm(h, ffn1_norm), ffn1_w_gate, ffn1_w_up, ffn1_w_down)

    u = rmsnorm(h, mix_norm)
    z = u @ w_in
    sizes = [2 * M_WIDTH, M_WIDTH, M_WIDTH, M_HEADS, M_HEADS, A_WIDTH, A_KV_WIDTH, A_KV_WIDTH, D_MODEL, D_MODEL]
    offs = [int(o) for o in np.cumsum(sizes)[:-1]]
    m_qk, m_v, m_o, m_i, m_f, a_q, a_k, a_v, g_m, g_a = jnp.split(z, offs, axis=-1)

    m_qk = jax.nn.silu(causal_dwconv(m_qk, m_conv_w, m_conv_b))
    m_q, m_k = jnp.split(m_qk, 2, axis=-1)
    mq = m_q.astype(jnp.float32).reshape(bsz, t, M_HEADS, M_HEAD_DIM) * (M_HEAD_DIM ** -0.5)
    mk = m_k.astype(jnp.float32).reshape(bsz, t, M_HEADS, M_HEAD_DIM)
    mv = m_v.astype(jnp.float32).reshape(bsz, t, M_HEADS, M_HEAD_DIM)
    ig = m_i.astype(jnp.float32) + m_igate_b.astype(jnp.float32)
    lf = jax.nn.log_sigmoid(m_f.astype(jnp.float32) + m_fgate_b.astype(jnp.float32))
    hm = mlstm_chunkwise(mq, mk, mv, ig, lf)
    hm = head_rmsnorm(hm, m_out_norm.reshape(M_HEADS, M_HEAD_DIM)).reshape(bsz, t, M_WIDTH)
    hm = (jax.nn.sigmoid(m_o.astype(jnp.float32)) * hm).astype(h.dtype)

    aq = head_rmsnorm(a_q.reshape(bsz, t, A_Q_HEADS, A_HEAD_DIM), a_q_norm).astype(h.dtype)
    ak = head_rmsnorm(a_k.reshape(bsz, t, A_KV_HEADS, A_HEAD_DIM), a_k_norm).astype(h.dtype)
    av = a_v.reshape(bsz, t, A_KV_HEADS, A_HEAD_DIM)
    ha = swa_gqa_sinks(aq, ak, av, a_sinks)

    merged = jax.nn.sigmoid(g_m) * (hm @ w_branch_m) + jax.nn.sigmoid(g_a) * (ha @ w_branch_a)
    h = h + merged @ w_out

    h = h + 0.5 * swiglu(rmsnorm(h, ffn2_norm), ffn2_w_gate, ffn2_w_up, ffn2_w_down)

    h = h + jax.nn.sigmoid(rmsnorm(h, ple_norm) @ ple_gate_w) * (p_i @ ple_proj_w)
    return h

def first_inputs(seed: int = 0) -> dict:
    key = jax.random.key(seed)
    ks = jax.random.split(key, 32)

    def w(k, fan_in, fan_out, scale=1.0):
        return jax.random.normal(k, (DEPTH, fan_in, fan_out), jnp.float32) * (scale * fan_in ** -0.5)

    def gain(k, n):
        return 1.0 + 0.05 * jax.random.normal(k, (DEPTH, n), jnp.float32)

    f_bias = jnp.linspace(3.0, 6.0, M_HEADS, dtype=jnp.float32)[None, :] + 0.1 * jax.random.normal(ks[10], (DEPTH, M_HEADS), jnp.float32)
    return {
        "x": jax.random.normal(ks[0], (BATCH, SEQ, D_MODEL), jnp.float32),
        "p": jax.random.normal(ks[1], (DEPTH, BATCH, SEQ, PLE_DIM), jnp.float32),
        "ffn1_norm": gain(ks[2], D_MODEL),
        "ffn1_w_gate": w(ks[3], D_MODEL, D_FF),
        "ffn1_w_up": w(ks[4], D_MODEL, D_FF),
        "ffn1_w_down": w(ks[5], D_FF, D_MODEL, 0.5),
        "mix_norm": gain(ks[6], D_MODEL),
        "w_in": w(ks[7], D_MODEL, N_IN),
        "m_conv_w": jax.random.normal(ks[8], (DEPTH, CONV_K, 2 * M_WIDTH), jnp.float32) * (CONV_K ** -0.5),
        "m_conv_b": 0.02 * jax.random.normal(ks[9], (DEPTH, 2 * M_WIDTH), jnp.float32),
        "m_igate_b": 0.1 * jax.random.normal(ks[11], (DEPTH, M_HEADS), jnp.float32),
        "m_fgate_b": f_bias,
        "m_out_norm": gain(ks[12], M_WIDTH),
        "a_q_norm": gain(ks[13], A_HEAD_DIM),
        "a_k_norm": gain(ks[14], A_HEAD_DIM),
        "a_sinks": 0.5 * jax.random.normal(ks[15], (DEPTH, A_Q_HEADS), jnp.float32),
        "w_branch_m": w(ks[16], M_WIDTH, D_MODEL),
        "w_branch_a": w(ks[17], A_WIDTH, D_MODEL),
        "w_out": w(ks[18], D_MODEL, D_MODEL, 0.5),
        "ffn2_norm": gain(ks[19], D_MODEL),
        "ffn2_w_gate": w(ks[20], D_MODEL, D_FF),
        "ffn2_w_up": w(ks[21], D_MODEL, D_FF),
        "ffn2_w_down": w(ks[22], D_FF, D_MODEL, 0.5),
        "ple_norm": gain(ks[23], D_MODEL),
        "ple_gate_w": w(ks[24], D_MODEL, D_MODEL),
        "ple_proj_w": w(ks[25], PLE_DIM, D_MODEL, 0.5),
    }

def first_block(x, p, ffn1_norm, ffn1_w_gate, ffn1_w_up, ffn1_w_down, mix_norm, w_in,
              m_conv_w, m_conv_b, m_igate_b, m_fgate_b, m_out_norm, a_q_norm, a_k_norm,
              a_sinks, w_branch_m, w_branch_a, w_out, ffn2_norm, ffn2_w_gate, ffn2_w_up,
              ffn2_w_down, ple_norm, ple_gate_w, ple_proj_w):
    h = x
    for i in range(DEPTH):
        h = hybrid_layer(h, p[i], ffn1_norm[i], ffn1_w_gate[i], ffn1_w_up[i], ffn1_w_down[i],
                         mix_norm[i], w_in[i], m_conv_w[i], m_conv_b[i], m_igate_b[i],
                         m_fgate_b[i], m_out_norm[i], a_q_norm[i], a_k_norm[i], a_sinks[i],
                         w_branch_m[i], w_branch_a[i], w_out[i], ffn2_norm[i], ffn2_w_gate[i],
                         ffn2_w_up[i], ffn2_w_down[i], ple_norm[i], ple_gate_w[i], ple_proj_w[i])
    return h


D_MIX = D_MODEL
A_DIM = D_MIX // 4
A_GROUPS = 4
A_CHUNK = 128
B_HEAD_DIM = 128
B_DIM = D_MIX // 2
B_HEADS = B_DIM // B_HEAD_DIM
B_CONV = 4
B_CHUNK = 64
C_HEAD_DIM = 64
C_DIM = D_MIX - A_DIM - B_DIM
C_HEADS = C_DIM // C_HEAD_DIM
C_CONFIGS = ((128, 1), (512, 4), (2048, 16))
C_QBLOCK = 128
ROPE_THETA = 10000.0
IN_SIZES = (A_DIM, A_DIM, 3 * B_DIM, B_DIM, B_HEADS, B_HEADS, C_DIM, C_DIM, C_DIM)
D_IN = sum(IN_SIZES)
D_FF_2 = ((8 * D_MODEL // 3 + 127) // 128) * 128
N_EXPERTS = 8
TOP_K = 2
N_DENSE = (DEPTH + 1) // 2
N_MOE = DEPTH // 2
DN_ALPHA = (2.0 * DEPTH) ** 0.25
DN_BETA = (8.0 * DEPTH) ** -0.25


def layer_norm(x, g, b, eps=1e-5):
    xf = x.astype(jnp.float32)
    mu = jnp.mean(xf, axis=-1, keepdims=True)
    var = jnp.mean(jnp.square(xf - mu), axis=-1, keepdims=True)
    return ((xf - mu) * lax.rsqrt(var + eps) * g + b).astype(x.dtype)

def rope(x):
    S, dh = x.shape[1], x.shape[-1]
    inv_freq = ROPE_THETA ** (-jnp.arange(0, dh, 2, dtype=jnp.float32) / dh)
    ang = jnp.arange(S, dtype=jnp.float32)[:, None] * inv_freq[None, :]
    cos = jnp.cos(ang)[None, :, None, :]
    sin = jnp.sin(ang)[None, :, None, :]
    x1 = x[..., : dh // 2].astype(jnp.float32)
    x2 = x[..., dh // 2:].astype(jnp.float32)
    return jnp.concatenate([x1 * cos - x2 * sin, x2 * cos + x1 * sin], axis=-1).astype(x.dtype)

def gmlp_spatial_gate(u, v, ln_g, ln_b, w_s, b_s):
    Bsz, S, _ = u.shape
    v = layer_norm(v, ln_g, ln_b)
    causal = jnp.tril(jnp.ones((A_CHUNK, A_CHUNK), dtype=bool))
    w = jnp.where(causal[None], w_s, jnp.zeros_like(w_s)).astype(v.dtype)
    vc = v.reshape(Bsz, S // A_CHUNK, A_CHUNK, A_GROUPS, A_DIM // A_GROUPS)
    mixed = jnp.einsum('gts,bnsgc->bntgc', w, vc) + b_s.T.astype(v.dtype)[None, None, :, :, None]
    return u * mixed.reshape(Bsz, S, A_DIM)

def causal_dwconv_2(x, w):
    K = w.shape[0]
    return lax.conv_general_dilated(
        x, w[:, None, :].astype(x.dtype), window_strides=(1,), padding=[(K - 1, 0)],
        dimension_numbers=('NWC', 'WIO', 'NWC'), feature_group_count=x.shape[-1])

def gated_deltanet(q, k, v, z, beta_logit, a_logit, a_log, dt_bias, norm_g):
    f32 = jnp.float32
    Bsz, S, _ = q.shape
    H, dk, C = B_HEADS, B_HEAD_DIM, B_CHUNK
    N = S // C
    q = q.reshape(Bsz, S, H, dk).astype(f32)
    k = k.reshape(Bsz, S, H, dk).astype(f32)
    v = v.reshape(Bsz, S, H, dk).astype(f32)
    q = q * lax.rsqrt(jnp.sum(q * q, -1, keepdims=True) + 1e-6) * (dk ** -0.5)
    k = k * lax.rsqrt(jnp.sum(k * k, -1, keepdims=True) + 1e-6)
    beta = jax.nn.sigmoid(beta_logit.astype(f32))
    g = -jnp.exp(a_log.astype(f32)) * jax.nn.softplus(a_logit.astype(f32) + dt_bias.astype(f32))

    def chunk(t):
        return t.reshape(Bsz, N, C, H, -1).transpose(0, 3, 1, 2, 4)

    qc, kc, vc = chunk(q), chunk(k), chunk(v)
    bc = chunk(beta[..., None])
    gc = jnp.cumsum(chunk(g[..., None])[..., 0], axis=-1)
    lower = jnp.tril(jnp.ones((C, C), dtype=bool))
    strict = jnp.tril(jnp.ones((C, C), dtype=bool), -1)
    decay = jnp.exp(jnp.where(lower, gc[..., :, None] - gc[..., None, :], -jnp.inf))
    k_beta = kc * bc
    m = jnp.where(strict, jnp.einsum('bhnid,bhnjd->bhnij', k_beta, kc) * decay, 0.0)
    eye = jnp.eye(C, dtype=f32)
    rhs = jnp.concatenate([vc * bc, k_beta * jnp.exp(gc)[..., None]], axis=-1)
    sol = lax.linalg.triangular_solve(eye + m, rhs, left_side=True, lower=True, unit_diagonal=True)
    u_c, w_c = sol[..., :dk], sol[..., dk:]
    attn_local = jnp.einsum('bhnid,bhnjd->bhnij', qc, kc) * decay
    q_dec = qc * jnp.exp(gc)[..., None]
    k_dec = kc * jnp.exp(gc[..., -1:] - gc)[..., None]
    g_last = jnp.exp(gc[..., -1])

    def step(state, xs):
        u_i, w_i, a_i, qd_i, kd_i, gl_i = xs
        v_new = u_i - jnp.einsum('bhcd,bhde->bhce', w_i, state)
        o = jnp.einsum('bhcd,bhde->bhce', qd_i, state) + jnp.einsum('bhij,bhje->bhie', a_i, v_new)
        state = state * gl_i[..., None, None] + jnp.einsum('bhcd,bhce->bhde', kd_i, v_new)
        return state, o

    xs = tuple(jnp.moveaxis(t, 2, 0) for t in (u_c, w_c, attn_local, q_dec, k_dec, g_last))
    _, o = lax.scan(step, jnp.zeros((Bsz, H, dk, dk), f32), xs)
    o = o.transpose(1, 0, 3, 2, 4).reshape(Bsz, S, H, dk)
    o = o * lax.rsqrt(jnp.mean(o * o, -1, keepdims=True) + 1e-6) * norm_g.astype(f32)
    o = o * jax.nn.silu(z.reshape(Bsz, S, H, dk).astype(f32))
    return o.reshape(Bsz, S, B_DIM).astype(z.dtype)

def dilated_attention(q, k, v):
    f32 = jnp.float32
    Bsz, S, H, dh = q.shape
    nblk = S // C_QBLOCK
    qb = (q * (dh ** -0.5)).reshape(Bsz, nblk, C_QBLOCK, H, dh).transpose(1, 0, 2, 3, 4)

    def block(args):
        blk, q_blk = args
        t = blk * C_QBLOCK + jnp.arange(C_QBLOCK)
        outs, lses = [], []
        for window, dil in C_CONFIGS:
            j = jnp.arange(window // dil + 1)
            idx = t[:, None] - dil * j[None, :]
            valid = idx >= 0
            idx = jnp.maximum(idx, 0)
            kg = jnp.take(k, idx, axis=1)
            vg = jnp.take(v, idx, axis=1)
            s = jnp.einsum('bqhd,bqjhd->bhqj', q_blk, kg).astype(f32)
            s = jnp.where(valid[None, None], s, -jnp.inf)
            mx = jnp.max(s, axis=-1, keepdims=True)
            e = jnp.exp(s - mx)
            den = jnp.sum(e, axis=-1)
            outs.append(jnp.einsum('bhqj,bqjhd->bqhd', e / den[..., None], vg.astype(f32)))
            lses.append(mx[..., 0] + jnp.log(den))
        wts = jax.nn.softmax(jnp.stack(lses, axis=0), axis=0)
        out = jnp.einsum('cbhq,cbqhd->bqhd', wts, jnp.stack(outs, axis=0))
        return out.astype(q_blk.dtype)

    out = lax.map(block, (jnp.arange(nblk), qb))
    return out.transpose(1, 0, 2, 3, 4).reshape(Bsz, S, H * dh)

def token_mixer(x, w_in, conv_w, a_ln_g, a_ln_b, a_ws, a_bs, b_a_log, b_dt_bias, b_norm_g, w_out):
    Bsz, S, _ = x.shape
    h = x @ w_in
    offs = [int(o) for o in np.cumsum(IN_SIZES)[:-1]]
    a_u, a_v, b_qkv, b_z, b_beta, b_a, c_q, c_k, c_v = jnp.split(h, offs, axis=-1)
    y_a = gmlp_spatial_gate(jax.nn.gelu(a_u), jax.nn.gelu(a_v), a_ln_g, a_ln_b, a_ws, a_bs)
    b_qkv = jax.nn.silu(causal_dwconv_2(b_qkv, conv_w))
    b_q, b_k, b_v = jnp.split(b_qkv, [B_DIM, 2 * B_DIM], axis=-1)
    y_b = gated_deltanet(b_q, b_k, b_v, b_z, b_beta, b_a, b_a_log, b_dt_bias, b_norm_g)
    cq = rope(c_q.reshape(Bsz, S, C_HEADS, C_HEAD_DIM))
    ck = rope(c_k.reshape(Bsz, S, C_HEADS, C_HEAD_DIM))
    cv = c_v.reshape(Bsz, S, C_HEADS, C_HEAD_DIM)
    y_c = dilated_attention(cq, ck, cv)
    return jnp.concatenate([y_a, y_b, y_c], axis=-1) @ w_out

def swiglu_2(x, w_gate, w_up, w_down):
    return (jax.nn.silu(x @ w_gate) * (x @ w_up)) @ w_down

def moe_swiglu(x, w_router, w_gate, w_up, w_down):
    Bsz, S, D = x.shape
    xt = x.reshape(Bsz * S, D)
    logits = (xt @ w_router).astype(jnp.float32)
    top_vals, top_idx = lax.top_k(logits, TOP_K)
    probs = jax.nn.softmax(top_vals, axis=-1)
    combine = jnp.sum(jax.nn.one_hot(top_idx, N_EXPERTS, dtype=jnp.float32) * probs[..., None], axis=1)

    def expert(acc, params):
        wg, wu, wd, c = params
        return acc + c[:, None].astype(xt.dtype) * swiglu_2(xt, wg, wu, wd), None

    acc, _ = lax.scan(expert, jnp.zeros_like(xt), (w_gate, w_up, w_down, combine.T))
    return acc.reshape(Bsz, S, D)

def second_inputs(seed: int = 0) -> dict:
    key = jax.random.key(seed)
    ks = jax.random.split(key, 24)
    nrm = jax.random.normal
    x = nrm(ks[0], (BATCH, SEQ, D_MODEL), jnp.float32)
    w_in = nrm(ks[1], (DEPTH, D_MODEL, D_IN), jnp.float32) * D_MODEL ** -0.5
    conv_w = nrm(ks[2], (DEPTH, B_CONV, 3 * B_DIM), jnp.float32) * B_CONV ** -0.5
    a_ln_g = 1.0 + 0.02 * nrm(ks[3], (DEPTH, A_DIM), jnp.float32)
    a_ln_b = 0.02 * nrm(ks[4], (DEPTH, A_DIM), jnp.float32)
    a_ws = nrm(ks[5], (DEPTH, A_GROUPS, A_CHUNK, A_CHUNK), jnp.float32) * A_CHUNK ** -0.5
    a_bs = 1.0 + 0.02 * nrm(ks[6], (DEPTH, A_GROUPS, A_CHUNK), jnp.float32)
    b_a_log = jnp.log(jax.random.uniform(ks[7], (DEPTH, B_HEADS), jnp.float32, 1.0, 16.0))
    dt = jnp.exp(jax.random.uniform(ks[8], (DEPTH, B_HEADS), jnp.float32, math.log(1e-3), math.log(1e-1)))
    b_dt_bias = dt + jnp.log(-jnp.expm1(-dt))
    b_norm_g = 1.0 + 0.02 * nrm(ks[9], (DEPTH, B_HEAD_DIM), jnp.float32)
    w_out = nrm(ks[10], (DEPTH, D_MIX, D_MODEL), jnp.float32) * (D_MIX ** -0.5) * DN_BETA
    ln1_g = 1.0 + 0.02 * nrm(ks[11], (DEPTH, D_MODEL), jnp.float32)
    ln1_b = 0.02 * nrm(ks[12], (DEPTH, D_MODEL), jnp.float32)
    ln2_g = 1.0 + 0.02 * nrm(ks[13], (DEPTH, D_MODEL), jnp.float32)
    ln2_b = 0.02 * nrm(ks[14], (DEPTH, D_MODEL), jnp.float32)
    ffn_w_gate = nrm(ks[15], (N_DENSE, D_MODEL, D_FF_2), jnp.float32) * D_MODEL ** -0.5
    ffn_w_up = nrm(ks[16], (N_DENSE, D_MODEL, D_FF_2), jnp.float32) * D_MODEL ** -0.5
    ffn_w_down = nrm(ks[17], (N_DENSE, D_FF_2, D_MODEL), jnp.float32) * (D_FF_2 ** -0.5) * DN_BETA
    moe_router = nrm(ks[18], (N_MOE, D_MODEL, N_EXPERTS), jnp.float32) * D_MODEL ** -0.5
    moe_w_gate = nrm(ks[19], (N_MOE, N_EXPERTS, D_MODEL, D_FF_2), jnp.float32) * D_MODEL ** -0.5
    moe_w_up = nrm(ks[20], (N_MOE, N_EXPERTS, D_MODEL, D_FF_2), jnp.float32) * D_MODEL ** -0.5
    moe_w_down = nrm(ks[21], (N_MOE, N_EXPERTS, D_FF_2, D_MODEL), jnp.float32) * (D_FF_2 ** -0.5) * DN_BETA
    return {"x": x, "w_in": w_in, "conv_w": conv_w, "a_ln_g": a_ln_g, "a_ln_b": a_ln_b,
            "a_ws": a_ws, "a_bs": a_bs, "b_a_log": b_a_log, "b_dt_bias": b_dt_bias,
            "b_norm_g": b_norm_g, "w_out": w_out, "ln1_g": ln1_g, "ln1_b": ln1_b,
            "ln2_g": ln2_g, "ln2_b": ln2_b, "ffn_w_gate": ffn_w_gate, "ffn_w_up": ffn_w_up,
            "ffn_w_down": ffn_w_down, "moe_router": moe_router, "moe_w_gate": moe_w_gate,
            "moe_w_up": moe_w_up, "moe_w_down": moe_w_down}

def second_block(x, w_in, conv_w, a_ln_g, a_ln_b, a_ws, a_bs, b_a_log, b_dt_bias, b_norm_g, w_out,
              ln1_g, ln1_b, ln2_g, ln2_b, ffn_w_gate, ffn_w_up, ffn_w_down,
              moe_router, moe_w_gate, moe_w_up, moe_w_down):
    for layer in range(DEPTH):
        mix = token_mixer(x, w_in[layer], conv_w[layer], a_ln_g[layer], a_ln_b[layer], a_ws[layer],
                          a_bs[layer], b_a_log[layer], b_dt_bias[layer], b_norm_g[layer], w_out[layer])
        x = layer_norm(DN_ALPHA * x + mix, ln1_g[layer], ln1_b[layer])
        i = layer // 2
        if layer % 2 == 0:
            f = swiglu_2(x, ffn_w_gate[i], ffn_w_up[i], ffn_w_down[i])
        else:
            f = moe_swiglu(x, moe_router[i], moe_w_gate[i], moe_w_up[i], moe_w_down[i])
        x = layer_norm(DN_ALPHA * x + f, ln2_g[layer], ln2_b[layer])
    return x


def setup_inputs(seed=0):
    out = dict(first_inputs(seed))
    for name, value in second_inputs(seed + 1).items():
        if name != "x":
            out[name + "_2"] = value
    return out


def reference(
    x, p, ffn1_norm, ffn1_w_gate, ffn1_w_up, ffn1_w_down, mix_norm, w_in, m_conv_w, m_conv_b,
    m_igate_b, m_fgate_b, m_out_norm, a_q_norm, a_k_norm, a_sinks, w_branch_m, w_branch_a,
    w_out, ffn2_norm, ffn2_w_gate, ffn2_w_up, ffn2_w_down, ple_norm, ple_gate_w, ple_proj_w,
    w_in_2, conv_w_2, a_ln_g_2, a_ln_b_2, a_ws_2, a_bs_2, b_a_log_2, b_dt_bias_2, b_norm_g_2,
    w_out_2, ln1_g_2, ln1_b_2, ln2_g_2, ln2_b_2, ffn_w_gate_2, ffn_w_up_2, ffn_w_down_2,
    moe_router_2, moe_w_gate_2, moe_w_up_2, moe_w_down_2,
):
    x = first_block(
        x, p, ffn1_norm, ffn1_w_gate, ffn1_w_up, ffn1_w_down, mix_norm, w_in, m_conv_w,
        m_conv_b, m_igate_b, m_fgate_b, m_out_norm, a_q_norm, a_k_norm, a_sinks, w_branch_m,
        w_branch_a, w_out, ffn2_norm, ffn2_w_gate, ffn2_w_up, ffn2_w_down, ple_norm, ple_gate_w,
        ple_proj_w,
    )
    return second_block(
        x, w_in_2, conv_w_2, a_ln_g_2, a_ln_b_2, a_ws_2, a_bs_2, b_a_log_2, b_dt_bias_2,
        b_norm_g_2, w_out_2, ln1_g_2, ln1_b_2, ln2_g_2, ln2_b_2, ffn_w_gate_2, ffn_w_up_2,
        ffn_w_down_2, moe_router_2, moe_w_gate_2, moe_w_up_2, moe_w_down_2,
    )


_drawn_inputs = setup_inputs


def setup_inputs(seed=0):
    import zlib

    import numpy as np

    out = dict(_drawn_inputs(seed))
    spreads = {}
    factors = {'ffn1_norm': 2.697,
     'm_conv_b': 8.0,
     'm_igate_b': 46.714,
     'm_out_norm': 3.387,
     'a_q_norm': 8.0,
     'a_k_norm': 6.312,
     'a_sinks': 31.293,
     'ple_norm': 4.234,
     'a_ln_g_2': 26.464,
     'a_ln_b_2': 25.271,
     'a_bs_2': 22.019,
     'b_norm_g_2': 7.558}
    for name, (base, spread) in spreads.items():
        noise = np.random.default_rng([zlib.crc32(name.encode()), seed]).standard_normal(out[name].shape)
        drawn = base * np.exp(spread * noise) if base else spread * noise
        out[name] = __import__('jax').numpy.asarray(drawn.astype(out[name].dtype))
    for name, factor in factors.items():
        out[name] = (out[name] * factor).astype(out[name].dtype)
    return out
```

```python
from contextlib import ExitStack, contextmanager
import numpy as np
import concourse.bass as bass
from concourse import mybir

F32 = mybir.dt.float32
F32R = mybir.dt.float32r
U32 = mybir.dt.uint32
ALU = mybir.AluOpType
ACT = mybir.ActivationFunctionType
AX = mybir.AxisListType

P = 128
T = 256
D = 1024
KT = D // P
LAYERS = 2
EPS = 1e-6
EPS_LN = 1e-5
BIG = 1e30
ALPHA = float((2.0 * LAYERS) ** 0.25)

SLAB = 2048
RAW = 3
SPLIT = 3
WIDE = 256
CHUNKS = 11

M_HEADS = 4
Q_HEADS = 16
KV_HEADS = 4
HEAD = 64
B_HEADS = 4
EXPERTS = 8


def ffn_stream(parts):
    chunks = [(g, u, d, at, c) for g, u, d, at in parts for c in range(CHUNKS)]
    out = []
    for i, (g, u, d, at, c) in enumerate(chunks):
        out += [(g, at, "cols", WIDE * c), (u, at, "cols", WIDE * c)]
        if i:
            _, _, d0, at0, c0 = chunks[i - 1]
            out.append((d0, at0, "rows", 2 * P * c0))
    _, _, d0, at0, c0 = chunks[-1]
    return out + [(d0, at0, "rows", 2 * P * c0)]


def cols(name, at, first, count):
    return [(name, at, "cols", first + WIDE * j) for j in range(count)]


QK0, V0, O0, I0, AQ0, AK0, AV0, GM0, GA0 = 0, 2048, 3072, 4096, 4104, 5128, 5384, 5640, 6664
AU1, AV1, QKV1, Z1, BETA1, CQ1, CK1, CV1 = 0, 256, 512, 2048, 2560, 2568, 2824, 3080


def layer1_stream(l):
    s = ffn_stream([("ffn1_w_gate", "ffn1_w_up", "ffn1_w_down", (l,))])
    s += cols("w_in", (l,), QK0, 8) + cols("w_in", (l,), V0, 4)
    s += cols("w_in", (l,), AQ0, 4) + cols("w_in", (l,), AK0, 1) + cols("w_in", (l,), AV0, 1)
    for i in range(M_HEADS + 2):
        if 1 <= i <= M_HEADS:
            s += cols("w_in", (l,), O0 + WIDE * (i - 1), 1)
        if i < M_HEADS:
            s += cols("w_in", (l,), GM0 + WIDE * i, 1) + cols("w_in", (l,), GA0 + WIDE * i, 1)
    s += cols("w_branch_m", (l,), 0, 4) + cols("w_branch_a", (l,), 0, 4) + cols("w_out", (l,), 0, 4)
    s += ffn_stream([("ffn2_w_gate", "ffn2_w_up", "ffn2_w_down", (l,))])
    s += cols("ple_gate_w", (l,), 0, 4) + [("ple_proj_w", (l,), "rows", 0)]
    return s


def layer2_stream(l):
    s = cols("w_in_2", (l,), QKV1, 6)
    for first in (AV1, AU1, CQ1, CK1, CV1, Z1, Z1 + WIDE):
        s += cols("w_in_2", (l,), first, 1)
    s += cols("w_out_2", (l,), 0, 4)
    if l == 0:
        s += ffn_stream([("ffn_w_gate_2", "ffn_w_up_2", "ffn_w_down_2", (0,))])
    else:
        s += ffn_stream([("moe_w_gate_2", "moe_w_up_2", "moe_w_down_2", (0, e)) for e in range(EXPERTS)])
    return s


def whole_stream():
    return [x for l in range(LAYERS) for x in layer1_stream(l)] + \
           [x for l in range(LAYERS) for x in layer2_stream(l)]


def param_columns():
    at, n = {}, 0
    for l in range(LAYERS):
        for name, w in (("ffn1_norm", 8), ("mix_norm", 8), ("m_conv_w", 64), ("m_conv_b", 16),
                        ("m_out_norm", 8), ("a_q_norm", 1), ("a_k_norm", 1), ("a_sinks", 16),
                        ("ffn2_norm", 8), ("ple_norm", 8), ("m_igate_b", 1), ("m_fgate_b", 1),
                        ("if_w", 64),
                        ("conv_w_2", 48), ("a_bs_2", 4), ("b_a_log_2", 1), ("b_dt_bias_2", 1),
                        ("b_norm_g_2", 1), ("ln1_g_2", 8), ("ln1_b_2", 8), ("ln2_g_2", 8),
                        ("ln2_b_2", 8), ("ba_w", 64)):
            at[name, l] = n
            n += w
    at["router", 0] = n
    return at, n + 64


CONST = {}
_n = 0
for _name, _w in (("ident", 128), ("tri", 128), ("iota", 8), ("blk", 128), ("swap", 128),
                  ("anti", 128), ("up", 128)):
    CONST[_name] = (_n, _w)
    _n += _w
N_CONST = _n
CONST2 = {}
_n = 0
for _name, _w in (("rot", 128), ("cos", 256), ("sin", 256), ("level", 7 * 128), ("causal", 128),
                  ("dmask", 3 * 128), ("dcount", 3 * 128)):
    CONST2[_name] = (_n, _w)
    _n += _w
N_CONST2 = _n


def constants():
    a = np.arange(P)
    row, col = a[:, None], a[None, :]
    one = np.zeros((P, N_CONST), np.float32)

    def put(t, where, name, v):
        o, w = where[name]
        t[:v.shape[0], o:o + w] = v

    put(one, CONST, "ident", np.eye(P))
    put(one, CONST, "blk", (row // 64 == col // 64) * 1.0)
    put(one, CONST, "swap", (row == (col + 64) % P) * 1.0)
    put(one, CONST, "iota", np.broadcast_to(np.arange(8.0), (P, 8)))
    put(one, CONST, "tri", np.where(row > col, BIG, 0.0))
    put(one, CONST, "up", np.where(col > row, -BIG, 0.0))
    put(one, CONST, "anti", np.where(col <= row, -BIG, 0.0))
    two = np.zeros((P, N_CONST2), np.float32)
    d = a % 64
    rot = np.zeros((P, P))
    for m in range(P):
        rot[m + 32 if d[m] < 32 else m - 32, m] = -1.0 if d[m] < 32 else 1.0
    put(two, CONST2, "rot", rot)
    inv = np.float32(10000.0) ** (-np.arange(0, 64, 2, dtype=np.float32) / np.float32(64))
    ang = np.arange(T, dtype=np.float32)[None, :] * inv[d % 32][:, None]
    put(two, CONST2, "cos", np.cos(ang))
    put(two, CONST2, "sin", np.sin(ang))
    lev = []
    for l in range(7):
        b = 1 << l
        lev.append(((row // (2 * b) == col // (2 * b)) & (col // b % 2 == 1) & (row // b % 2 == 0)) * 1.0)
    put(two, CONST2, "level", np.concatenate(lev, 1))
    put(two, CONST2, "causal", (row <= col) * 1.0)
    masks, counts = [], []
    for b, kb in ((0, 0), (1, 0), (1, 1)):
        rel = (b * P + row) - (kb * P + col)
        n = ((rel >= 0) & (rel <= 128)) * 1.0 + ((rel >= 0) & (rel % 4 == 0) & (rel <= 512)) \
            + ((rel >= 0) & (rel % 16 == 0))
        masks.append(np.where(n > 0, 0.0, -BIG))
        counts.append(n)
    put(two, CONST2, "dmask", np.concatenate(masks, 1))
    put(two, CONST2, "dcount", np.concatenate(counts, 1))
    return one, two


class Count:

    def __init__(self, eng, slabs):
        self.eng, self.slabs = eng, slabs
        self.n, self.i, self.per = {}, None, {}
        self.block = 0

    def get(self, key):
        return self.n.get(key, 0)

    def add(self, key, k=1):
        self.n[key] = self.get(key) + k
        return self.n[key]

    def at(self, name, value):
        assert value > 0, name
        return value if self.i is None else self.i * self.per[name] + value

    def next(self, name, k=1):
        return self.at(name, self.add(("seen", name), k))

    def one(self, name):
        self.add(("made", name))
        return 1

    def own(self, name):
        return self.at(name, self.get(("made", name)))

    def slab(self):
        return self.add("slab") - 1

    def due(self):
        m = []
        while self.get("conv") <= self.get("slab") + 1 and (self.i is not None or self.get("conv") < self.slabs):
            m.append(self.add("conv") - 1)
        return m

    @contextmanager
    def turns(self, count, per):
        before = dict(self.n)
        with self.eng.Fori(0, count) as i:
            self.i, self.per = i, per
            yield i
        self.i = None
        for key in self.n:
            gained = self.n[key] - before.get(key, 0)
            name = key[1] if isinstance(key, tuple) else key
            assert gained in (0, per.get(name)), (key, gained, per.get(name))
            self.n[key] = before.get(key, 0) + gained * count


RESID_PER_LAYER = 16

SEMS = """slab_in0 slab_in1 slab_in2 hi_done lo_dve lo_pool slab_used setup_in setup_done p_in
act_step dve_step act_full dve_full act_free dve_free
sq_ready std_ready std_taken x2_ready resid sil_ready h_mul h_ready
gate_abs gate_ln rows_ready conv_done qk_ready sqa_ready an_ready
arg_ready w_ready s_ready den_ready hm_ready sqm_ready sigo_ready hm_split sg_ready gated x2m_ready
sc_masked nmx_ready exp_ready p_ready pt_ready ha_ready psplit_ready out_done
tab_in gmlp_in gv_arg gv_std top_logits col_ready bc_ready dt_arg dt_ready ec_arg ec_ready g_ready xt_ready x_new ml_ready y_ready
gelu_ready gv_ready ya_ready yp_ready cqk_ready rope_ready silz_ready qd_arg qd_exp qd_ready rv_ready u_ready wt_ready
st_ready o_ready vn_ready top_arg top_exp comb_ready ct_ready cbc_ready ln_done""".split()


FFN_TURN = {"slab": 6, "conv": 6, "hi_done": 6, "lo_dve": 6, "lo_pool": 6, "slab_used": 6,
            "act_unit": 2, "dve_unit": 2, "sil_ready": 2, "h_mul": 2, "h_ready": 2, "chunk": 2,
            "dve_step": 2, "slab_in0": 32, "slab_in1": 32, "slab_in2": 32}


def build(nc, stream, x_t, p_t, params, const, const2, gmlp_w, out, layers1=LAYERS, layers2=LAYERS):
    n_slabs = stream.shape[0]
    PAR, n_par = param_columns()
    ctx = ExitStack()
    with ctx:
        def sb(name, width, dt=F32):
            return ctx.enter_context(nc.sbuf_tensor(name, [P, width], dt))

        def ps(name, banks):
            return ctx.enter_context(nc.psum_tensor(name, [P, banks, 512], F32))

        S = {name: ctx.enter_context(nc.semaphore(name)) for name in SEMS}

        raw = sb("raw", RAW * SLAB)
        wh = sb("wh", SPLIT * SLAB, F32R)
        wl = sb("wl", SPLIT * SLAB, F32R)
        hT = sb("hT", KT * T)
        U = sb("U", KT * T)
        x2 = sb("x2", 2 * KT * T, F32R)
        x2m = sb("x2m", 2 * KT * T, F32R)
        h2 = sb("h2", 2 * 2 * 2 * T, F32R)
        con = sb("con", N_CONST)
        par = sb("par", n_par)
        ones = sb("ones", T)
        eps = sb("eps", 2)
        MIXW = 18560
        mix = sb("mix", MIXW)

        acc = ps("acc", 4)
        actb = ps("actb", 2)
        dveb = ps("dveb", 2)
        bank_of = {"act": actb, "dve": dveb}

        def tiles(t, n=KT, w=T):
            return t[:, 0:n * w].rearrange("p (k t) -> p k t", k=n)

        hT3, U3 = tiles(hT), tiles(U)
        x2v = x2[:, :].rearrange("p (s k t) -> p s k t", s=2, k=KT)
        x2mv = x2m[:, :].rearrange("p (s k t) -> p s k t", s=2, k=KT)
        h2v = h2[:, :].rearrange("p (b s k t) -> p b s k t", b=2, s=2, k=2)

        def asf(ap):
            return ap.bitcast(F32)

        def c1(name, rows=P, first=0, width=None):
            o, w = CONST[name]
            return con[0:rows, o + first:o + first + (width or w)]

        def prm(name, l, k=0, w=1, rows=P):
            o = PAR[name, l] + k
            return par[0:rows, o:o + w]

        off = [0]

        def cut(width, at=None):
            o = off[0] if at is None else at
            if at is None:
                off[0] += width
            assert o + width <= MIXW, (o, width)
            return mix[:, o:o + width]

        qkc = cut(16 * T)
        aq = cut(8 * T)
        ak = cut(2 * T)
        aks = cut(2 * T)
        av = cut(2 * T)
        sgm = cut(8 * T)
        sga = cut(8 * T)
        sigo = cut(2 * 2 * T)
        warg = cut(2 * 640)
        Sw = cut(2 * 384)
        dn = cut(T)
        hm = cut(2 * 2 * T)
        sqm = cut(2 * 2 * T)
        std = acc[:, 2:4, :].rearrange("p b t -> p (b t)")
        rinv = cut(2 * T)
        gcol = cut(8)
        small = cut(64)
        rows8 = sga
        MM = sgm[:, 6 * T:8 * T]
        cacc = sqm
        sqa = hm
        scb = cut(2 * 1024, at=0)
        ptb = cut(2 * 1024, at=2048)
        sil = cut(2 * 512, at=0)
        hf = cut(2 * 512, at=1024)
        pf = cut(2 * T, at=2048)
        tmp = cut(2 * T, at=2048 + 512)

        tab = cut(N_CONST2, at=0)
        gmw = cut(1024, at=2432)
        qkvc = cut(12 * T, at=3456)
        BC = cut(4 * 2 * T, at=6528)
        DT = cut(8 * P, at=8576)
        AT = cut(8 * P, at=9600)
        XT = cut(8 * P, at=10624)
        MT = cut(8 * P, at=11648)
        X = cut(8 * P, at=12672)
        Y = cut(8 * P, at=13696)
        MLT = cut(8 * P, at=14720)
        utok = cut(2 * T, at=15744)
        gtok = cut(2 * T, at=16256)
        cqk = cut(4 * T, at=16768)
        col = cut(16, at=17792)
        sm2 = cut(32, at=17808)
        small2 = cut(64, at=17840)
        comb = cut(96, at=17904)
        rinv2 = cut(512, at=18048)
        cv = con[:, CONST["blk"][0]:CONST["blk"][0] + 2 * T]
        rows2 = X
        rows2b = Y
        cacc2 = MLT
        RV, RK, KD = DT, X[:, 0:512], X[:, 512:1024]
        Uc, St, WT = MT, Y[:, 0:512], Y[:, 512:1024]
        VN, QD = MLT[:, 0:512], MLT[:, 512:1024]
        OT, silz = U[:, 0:1024], U[:, 1024:2048]
        sqo = MT
        scb2 = BC
        ptb2 = qkvc[:, 0:2048]
        sil2, hf2 = DT, AT
        cbc = cut(8 * T, at=10624)
        ixb = ctx.enter_context(nc.sbuf_tensor("ixb", [P, 16], U32))
        SCB, PTB, SMALL, SIL, HF, CACC, QKC = ([a, b] for a, b in (
            (scb, scb2), (ptb, ptb2), (small, small2), (sil, sil2), (hf, hf2), (cacc, cacc2), (qkc, qkvc)))

        def t2(name, first=0, width=None):
            o, w = CONST2[name]
            return tab[:, o + first:o + first + (width or w)]

        def g4(t):
            return t.rearrange("p (h t) -> p h t", h=4)

        vtok = U[:, :].rearrange("p (s f) -> p s f", s=2)

        block = ctx.enter_context(nc.Block())

        @block.sync
        def _(sp):
            c = Count(sp, n_slabs)
            sp.dma_start(hT3, x_t).then_inc(S["setup_in"], 16)
            sp.dma_start(par[:, :], params).then_inc(S["setup_in"], 16)
            sp.dma_start(con[:, :], const).then_inc(S["setup_in"], 16)
            raw3 = raw[:, :].rearrange("p (r f) -> p r f", r=RAW)
            for r in range(RAW):
                sp.dma_start(raw3[:, r, :], stream[r]).then_inc(S[f"slab_in{r}"], 16)

            def load(n, r):
                sp.wait_ge(S["lo_dve"], n - RAW + 1)
                sp.wait_ge(S["lo_pool"], n - RAW + 1)
                sp.dma_start(raw3[:, r, :], stream[n]).then_inc(S[f"slab_in{r}"], 16)

            turns = n_slabs // RAW
            with sp.Fori(1, turns) as i:
                for r in range(RAW):
                    load(i * RAW + r, r)
            for n in range(turns * RAW, n_slabs):
                load(n, n % RAW)
            sp.wait_ge(S["resid"], RESID_PER_LAYER * layers1 + 8 * layers2)
            if layers2:
                sp.wait_ge(S["ln_done"], 2 * layers2)
            sp.dma_start(out, hT3).then_inc(S["out_done"], 16)
            sp.wait_ge(S["out_done"], 16)

        HALF = SLAB // 2

        @block.gpsimd
        def _(pool):
            c = Count(pool, n_slabs)
            nc.gpsimd.memset(ones[:, :], 1.0)
            nc.gpsimd.memset(eps[:, 0:1], EPS)
            nc.gpsimd.memset(eps[:, 1:2], EPS_LN).then_inc(S["setup_done"], 1)

            def split_lo(m):
                r, d = m % RAW * SLAB + HALF, m % SPLIT * SLAB + HALF
                pool.wait_ge(S["hi_done"], c.at("hi_done", m + 1))
                nc.gpsimd.tensor_tensor(wl[:, d:d + HALF], raw[:, r:r + HALF], asf(wh[:, d:d + HALF]),
                                        ALU.subtract).then_inc(S["lo_pool"], c.one("lo_pool"))

            turns = n_slabs // RAW
            with c.turns(turns, {"hi_done": RAW, "lo_pool": RAW}):
                for m in range(RAW):
                    split_lo(m)
            for m in range(turns * RAW, n_slabs):
                split_lo(m)

        @block.tensor
        def _(pe):
            c = Count(pe, n_slabs)
            owner = {}

            def mm(out, lhs, rhs, start, stop):
                return pe.matmul(out, lhs, rhs, start=start, stop=stop, skip_group_check=True)

            def mm3(out, lh, ll, rh, rl, start, stop):
                mm(out, lh, rh, start, False)
                mm(out, lh, rl, False, False)
                return mm(out, ll, rh, False, stop)

            def unit(who, freed_by):
                k = c.get(who + "_unit")
                c.add(who + "_unit")
                if (who, k % 2) in owner:
                    name, v = owner[who, k % 2]
                    pe.wait_ge(S[name], c.at(name, v))
                owner[who, k % 2] = (freed_by, c.add(("frees", freed_by)))
                return bank_of[who][:, k % 2, :]

            def slab():
                n = c.get("slab")
                c.add("slab")
                pe.wait_ge(S["hi_done"], c.at("hi_done", n + 1))
                pe.wait_ge(S["lo_dve"], c.at("lo_dve", n + 1))
                pe.wait_ge(S["lo_pool"], c.at("lo_pool", n + 1))
                s = n % SPLIT
                return wh[:, s * SLAB:(s + 1) * SLAB], wl[:, s * SLAB:(s + 1) * SLAB]

            def project(who, freed_by, x=x2v, tokens=False):
                if tokens:
                    return project_tokens(who, freed_by)
                bank = unit(who, freed_by)
                h, l = slab()
                for m in range(2):
                    for k in range(KT):
                        a = k * WIDE + m * P
                        last = mm3(bank[:, m * T:(m + 1) * T], h[:, a:a + P], l[:, a:a + P],
                                   x[:, 0, k, :], x[:, 1, k, :], k == 0, k == KT - 1)
                last.then_inc(S["slab_used"], 1)

            def project_tokens(who, freed_by):
                bank = unit(who, freed_by)
                h, l = slab()
                for m in range(2):
                    for k in range(KT):
                        last = mm3(bank[:, m * T:(m + 1) * T],
                                   x2v[:, 0, k, m * P:(m + 1) * P], x2v[:, 1, k, m * P:(m + 1) * P],
                                   h[:, k * WIDE:(k + 1) * WIDE], l[:, k * WIDE:(k + 1) * WIDE],
                                   k == 0, k == KT - 1)
                last.then_inc(S["slab_used"], 1)

            def pick_row(rows, i):
                return c1("ident", rows, i, 1).to_broadcast([rows, P])

            def norm_sum():
                pe.wait_ge(S["sq_ready"], c.next("sq_ready"))
                bank = unit("act", "std_ready")
                for k in range(KT):
                    last = mm(bank[:, 0:T], ones[:, 0:P], U3[:, k, :], k == 0, k == KT - 1)
                last.then_inc(S["act_full"], 1)

            def down(first, last_chunk):
                k = c.get("chunk")
                c.add("chunk")
                h, l = slab()
                pe.wait_ge(S["h_ready"], c.next("h_ready"))
                for f in range(2):
                    for m in range(KT):
                        a = f * D + m * P
                        last = mm3(acc[:, m // 2, (m % 2) * T:(m % 2 + 1) * T], h[:, a:a + P], l[:, a:a + P],
                                   h2v[:, k % 2, 0, f, :], h2v[:, k % 2, 1, f, :],
                                   first and f == 0 and m % 2 == 0, last_chunk and f == 1)
                last.then_inc(S["slab_used"], 1)

            def ffn(chunks):
                pe.wait_ge(S["x2_ready"], c.next("x2_ready"))

                def step(k):
                    project("act", "sil_ready")
                    project("dve", "h_mul")
                    if k:
                        down(k == 1, False)
                step(0)
                step(1)
                with c.turns((chunks - 3) // 2, FFN_TURN):
                    step(2)
                    step(3)
                for q in ("act", "dve"):
                    for b in range(2):
                        name, v = owner[q, b]
                        owner[q, b] = (name, v + 2 * ((chunks - 3) // 2 - 1))
                for k in range(2 + (chunks - 3) // 2 * 2, chunks):
                    step(k)
                down(False, True)
                c.add(("frees", "resid"), 4)

            def norm_heads(pair_event):
                pe.wait_ge(S[pair_event], c.next(pair_event))
                bank = unit("act", "std_ready")
                k = c.add("sqa") - 1
                mm(bank, c1("blk"), sqa[:, (k % 2) * 512:(k % 2 + 1) * 512], True, True).then_inc(S["act_full"], 1)

            def layer1(l):
                norm_sum()
                ffn(CHUNKS)
                norm_sum()
                pe.wait_ge(S["x2_ready"], c.next("x2_ready"))
                bank = unit("dve", "dve_free")
                for part in range(2):
                    for k in range(KT):
                        last = mm(bank[0:4, part * T:(part + 1) * T],
                                  prm("if_w", l, k * 8 + part * 4, 4), U3[:, k, :], k == 0, k == KT - 1)
                last.then_inc(S["dve_full"], 1)
                for j in range(8):
                    project("dve", "conv_done")
                    if j == 3:
                        pe.wait_ge(S["rows_ready"], c.next("rows_ready"))
                        bank = unit("act", "act_free")
                        for ch in range(2):
                            last = pe.transpose(bank[:, ch * 4:ch * 4 + 4],
                                                rows8[0:4, 7 * T + ch * P:7 * T + (ch + 1) * P], c1("ident", 4, 0, 4))
                        last.then_inc(S["act_full"], 1)
                for j in range(4):
                    project_tokens("act", "act_free")
                for j in range(4):
                    project("act", "sqa_ready")
                    if j:
                        norm_heads("sqa_ready")
                project("act", "sqa_ready")
                norm_heads("sqa_ready")
                project_tokens("act", "act_free")
                norm_heads("sqa_ready")
                pe.wait_ge(S["an_ready"], c.next("an_ready", 5))
                bank = unit("dve", "dve_free")
                mm(bank, c1("swap"), ak, True, True).then_inc(S["dve_full"], 1)

                for i in range(M_HEADS + 2):
                    if 1 <= i <= M_HEADS:
                        project("act", "sigo_ready")
                    if i < M_HEADS:
                        bank = unit("dve", "arg_ready")
                        mm(bank, pick_row(4, i), MM[0:4, :], True, True).then_inc(S["dve_full"], 1)
                    if 1 <= i <= M_HEADS:
                        h, b = i - 1, (i - 1) % 2
                        pe.wait_ge(S["s_ready"], c.next("s_ready"))
                        s0, s1 = Sw[:, b * 384:b * 384 + T], Sw[:, b * 384 + T:b * 384 + 384]
                        bank = unit("dve", "hm_ready")
                        for vt in range(2):
                            f = h * T + vt * P
                            mm(bank[:, vt * T:(vt + 1) * T], vtok[:, 0, f:f + P], s0, True, False)
                            last = mm(bank[:, vt * T + P:(vt + 1) * T], vtok[:, 1, f:f + P], s1, False, True)
                        last.then_inc(S["dve_full"], 1)
                        bank = unit("act", "den_ready")
                        mm(bank[:, 0:T], ones[:, 0:P], s0, True, False)
                        mm(bank[:, P:T], ones[:, 0:P], s1, False, True).then_inc(S["act_full"], 1)
                    if i < M_HEADS:
                        project("act", "sg_ready")
                        bank = unit("dve", "s_ready")
                        q = tiles(qkc, 16)[:, 2 * i:2 * i + 2, :]
                        kk = tiles(qkc, 16)[:, 8 + 2 * i:10 + 2 * i, :]
                        for k in range(2):
                            mm(bank[:, 0:T], kk[:, k, 0:P], q[:, k, :], k == 0, k == 1)
                        for k in range(2):
                            last = mm(bank[:, T:T + P], kk[:, k, P:T], q[:, k, P:T], k == 0, k == 1)
                        last.then_inc(S["dve_full"], 1)
                        project("act", "sg_ready")
                    if i >= 2:
                        b = i % 2
                        pe.wait_ge(S["sqm_ready"], c.next("sqm_ready"))
                        bank = unit("act", "std_ready")
                        mm(bank[:, 0:T], ones[:, 0:P], sqm[:, b * 512:b * 512 + T], True, False)
                        mm(bank[:, 0:T], ones[:, 0:P], sqm[:, b * 512 + T:b * 512 + 512], False, True)\
                            .then_inc(S["act_full"], 1)
                pe.wait_ge(S["hm_split"], c.next("hm_split", 4))
                items = [(g, b) for g in range(KV_HEADS) for b in range(2)]
                for i in range(len(items) + 2):
                    if i < 4:
                        project("dve", "gated", x2mv)
                    if i < len(items):
                        g, b = items[i]
                        scores(b, lambda hh: aq[:, (2 * g + hh // 2) * T:(2 * g + hh // 2 + 1) * T],
                               lambda hh: (ak if g % 2 == hh % 2 else aks)[:, (g // 2) * T:(g // 2 + 1) * T])
                    if 1 <= i <= len(items):
                        turn_probs(i - 1, items[i - 1][1] + 1)
                    if i >= 2:
                        g, b = items[i - 2]
                        attend(i - 2, b + 1, lambda hh: g, av)
                pe.wait_ge(S["ha_ready"], c.at("ha_ready", 8 * (l + 1)))
                for j in range(4):
                    project("dve", "gated")
                pe.wait_ge(S["x2m_ready"], c.at("x2m_ready", 4 * (l + 1)))
                for j in range(4):
                    project("dve", "resid", x2mv)
                norm_sum()
                ffn(CHUNKS)
                norm_sum()
                pe.wait_ge(S["x2_ready"], c.next("x2_ready"))
                for j in range(4):
                    project("act", "sg_ready")
                pe.wait_ge(S["psplit_ready"], c.next("psplit_ready"))
                h, lo = slab()
                for j in range(4):
                    bank = unit("dve", "gated")
                    for m in range(2):
                        for k in range(2):
                            a = k * D + (2 * j + m) * P
                            last = mm3(bank[:, m * T:(m + 1) * T], h[:, a:a + P], lo[:, a:a + P],
                                       h2v[:, 0, 0, k, :], h2v[:, 0, 1, k, :], k == 0, k == 1)
                    last.then_inc(S["dve_full" if j < 3 else "slab_used"], 1)
                c.add(("frees", "resid"), 4)

            def scores(b, q, k):
                n = (b + 1) * P
                for half in range(2):
                    r = slice(half * HEAD, (half + 1) * HEAD)
                    bank = unit("dve", "sc_masked")
                    for j in range(2):
                        hh = 2 * j + half
                        last = mm(bank[:, j * n:(j + 1) * n], q(hh)[r, b * P:(b + 1) * P], k(hh)[r, 0:n], True, True)
                    last.then_inc(S["dve_full"], 1)

            def turn_probs(i, nk):
                pe.wait_ge(S["p_ready"], c.next("p_ready"))
                for kb in range(nk):
                    bank = unit("act", "pt_ready")
                    sc = SCB[c.block][:, (i % 2) * 1024:(i % 2) * 1024 + 4 * nk * P].rearrange("p (h k) -> p h k", h=4)
                    for hh in range(4):
                        last = pe.transpose(bank[:, hh * P:(hh + 1) * P], sc[:, hh, kb * P:(kb + 1) * P], c1("ident"))
                    last.then_inc(S["act_full"], 1)

            def attend(i, nk, kv, v):
                pe.wait_ge(S["pt_ready"], c.next("pt_ready", nk))
                bank = unit("dve", "ha_ready")
                pt = PTB[c.block][:, (i % 2) * 1024:(i % 2 + 1) * 1024]
                for hh in range(4):
                    r = (hh % 2) * HEAD
                    for kb in range(nk):
                        last = mm(bank[r:r + HEAD, (hh // 2) * P:(hh // 2 + 1) * P],
                                  v[:, kb * T + kv(hh) * HEAD:kb * T + (kv(hh) + 1) * HEAD],
                                  pt[:, kb * 512 + hh * P:kb * 512 + (hh + 1) * P], kb == 0, kb == nk - 1)
                last.then_inc(S["dve_full"], 1)

            def four(bank, lhs, rhs):
                for h in range(4):
                    last = mm(bank[:, h * P:(h + 1) * P], lhs(h), rhs(h), True, True)
                return last

            def ph(t, ch, h):
                return t[:, (4 * ch + h) * P:(4 * ch + h + 1) * P]

            def at_chunk(t, tile, ch):
                return t[:, tile * T + ch * P:tile * T + (ch + 1) * P]

            def norm_pair(src):
                bank = unit("act", "std_ready")
                mm(bank, ones[:, 0:P], src, True, True).then_inc(S["act_full"], 1)

            def layer2(l):
                pe.wait_ge(S["x2_ready"], c.next("x2_ready"))
                bank = unit("dve", "dve_free")
                for part in range(2):
                    for k in range(KT):
                        last = mm(bank[0:4, part * T:(part + 1) * T],
                                  prm("ba_w", l, k * 8 + part * 4, 4), hT3[:, k, :], k == 0, k == KT - 1)
                last.then_inc(S["dve_full"], 1)
                for j in range(6):
                    project("dve", "conv_done")
                    if j >= 2:
                        pe.wait_ge(S["sq_ready"], c.next("sq_ready"))
                        norm_pair(U[:, (j - 2) * 512:(j - 1) * 512])
                    if j == 3:
                        pe.wait_ge(S["rows_ready"], c.next("rows_ready"))
                        bank = unit("act", "col_ready")
                        for ch in range(2):
                            for part in range(2):
                                last = pe.transpose(bank[:, (2 * ch + part) * 4:(2 * ch + part + 1) * 4],
                                                    rows2[0:4, part * T + ch * P:part * T + (ch + 1) * P],
                                                    c1("ident", 4, 0, 4))
                        last.then_inc(S["act_full"], 1)
                        for h in range(4):
                            bank = unit("dve", "bc_ready")
                            mm(bank, pick_row(4, h), rows2[0:4, 0:512], True, True).then_inc(S["dve_full"], 1)
                project("act", "gelu_ready", x2v, tokens=True)
                pe.wait_ge(S["an_ready"], c.next("an_ready", 4))
                for ch in range(2):
                    bank = unit("dve", "g_ready")
                    four(bank, lambda h: at_chunk(qkvc, 4 + h, ch), lambda h: at_chunk(qkvc, 4 + h, ch))\
                        .then_inc(S["dve_full"], 1)
                    bank = unit("dve", "g_ready")
                    four(bank, lambda h: at_chunk(qkvc, 4 + h, ch), lambda h: at_chunk(qkvc, h, ch))\
                        .then_inc(S["dve_full"], 1)
                for ch in range(2):
                    pe.wait_ge(S["xt_ready"], c.next("xt_ready"))
                    bank = unit("dve", "x_new")
                    for h in range(4):
                        last = pe.transpose(bank[:, h * P:(h + 1) * P], ph(XT, ch, h), c1("ident"))
                    last.then_inc(S["dve_full"], 1)
                pe.wait_ge(S["x_new"], c.next("x_new", 2))
                for level in range(1, 7):
                    for ch in range(2):
                        pe.wait_ge(S["ml_ready"], c.next("ml_ready"))
                        bank = unit("act", "y_ready")
                        four(bank, lambda h: ph(MLT, ch, h), lambda h: ph(X, ch, h)).then_inc(S["act_full"], 1)
                    if level in (1, 4):
                        project("act", "gelu_ready" if level == 1 else "cqk_ready", x2v, tokens=True)
                    elif level in (2, 3):
                        project("act", "cqk_ready")
                    else:
                        project("act", "silz_ready")
                    if level == 4:
                        pe.wait_ge(S["gv_ready"], c.next("gv_ready"))
                        bank = unit("dve", "ya_ready")
                        for tt in range(2):
                            for g in range(4):
                                last = mm(bank[:, tt * T + g * HEAD:tt * T + (g + 1) * HEAD],
                                          gmw[:, g * P:(g + 1) * P],
                                          gtok[:, tt * T + g * HEAD:tt * T + (g + 1) * HEAD], True, True)
                        last.then_inc(S["dve_full"], 1)
                    if level == 5:
                        pe.wait_ge(S["ya_ready"], c.next("ya_ready"))
                        bank = unit("dve", "yp_ready")
                        for ft in range(2):
                            for tt in range(2):
                                last = pe.transpose(bank[:, ft * T + tt * P:ft * T + (tt + 1) * P],
                                                    utok[:, tt * T + ft * P:tt * T + (ft + 1) * P], c1("ident"))
                        last.then_inc(S["dve_full"], 1)
                    if level == 6:
                        pe.wait_ge(S["cqk_ready"], c.next("cqk_ready", 3))
                        for j in range(2):
                            bank = unit("dve", "rope_ready")
                            mm(bank, t2("rot"), cqk[:, j * 512:(j + 1) * 512], True, True).then_inc(S["dve_full"], 1)
                    for ch in range(2):
                        pe.wait_ge(S["y_ready"], c.next("y_ready"))
                        if level < 6:
                            bank = unit("dve", "x_new")
                            four(bank, lambda h: ph(XT, ch, h), lambda h: ph(Y, ch, h)).then_inc(S["dve_full"], 1)
                        bank = unit("dve", "x_new")
                        four(bank, lambda h: ph(Y, ch, h), lambda h: ph(XT, ch, h)).then_inc(S["dve_full"], 1)
                    pe.wait_ge(S["x_new"], c.next("x_new", 4 if level < 6 else 2))
                for src, ch in ((8, 0), (8, 1), (4, 0), (4, 1)):
                    bank = unit("dve", "rv_ready")
                    for h in range(4):
                        last = pe.transpose(bank[:, h * P:(h + 1) * P], at_chunk(qkvc, src + h, ch), c1("ident"))
                    last.then_inc(S["dve_full"], 1)
                pe.wait_ge(S["rv_ready"], c.next("rv_ready", 2))
                for ch in range(2):
                    bank = unit("dve", "u_ready")
                    four(bank, lambda h: ph(XT, ch, h), lambda h: ph(RV, ch, h)).then_inc(S["dve_full"], 1)
                pe.wait_ge(S["rv_ready"], c.next("rv_ready", 2))
                hh = lambda t, h: t[:, h * P:(h + 1) * P]
                bank = unit("act", "wt_ready")
                four(bank, lambda h: hh(RK, h), lambda h: ph(XT, 1, h)).then_inc(S["act_full"], 1)
                pe.wait_ge(S["u_ready"], c.next("u_ready", 2))
                bank = unit("act", "st_ready")
                four(bank, lambda h: hh(KD, h), lambda h: ph(Uc, 0, h)).then_inc(S["act_full"], 1)
                bank = unit("dve", "o_ready")
                four(bank, lambda h: ph(Uc, 0, h), lambda h: ph(AT, 0, h)).then_inc(S["dve_full"], 1)
                pe.wait_ge(S["wt_ready"], c.next("wt_ready"))
                pe.wait_ge(S["st_ready"], c.next("st_ready"))
                bank = unit("dve", "vn_ready")
                four(bank, lambda h: hh(WT, h), lambda h: hh(St, h)).then_inc(S["dve_full"], 1)
                pe.wait_ge(S["vn_ready"], c.next("vn_ready"))
                pe.wait_ge(S["qd_ready"], c.next("qd_ready"))
                bank = unit("dve", "o_ready")
                for h in range(4):
                    mm(hh(bank, h), hh(St, h), hh(QD, h), True, False)
                    last = mm(hh(bank, h), hh(VN, h), ph(AT, 1, h), False, True)
                last.then_inc(S["dve_full"], 1)
                pe.wait_ge(S["sq_ready"], c.next("sq_ready"))
                for j in range(2):
                    norm_pair(sqo[:, j * 512:(j + 1) * 512])
                for i in range(2 + 2):
                    if i < 2:
                        if i == 0:
                            pe.wait_ge(S["rope_ready"], c.next("rope_ready", 2))
                        scores(i, lambda hh: cqk[:, (hh // 2) * T:(hh // 2 + 1) * T],
                               lambda hh: cqk[:, (2 + hh // 2) * T:(3 + hh // 2) * T])
                    if 1 <= i <= 2:
                        turn_probs(i - 1, i)
                    if i >= 2:
                        attend(i - 2, i - 1, lambda hh: hh, cv)
                pe.wait_ge(S["ha_ready"], c.at("ha_ready", 8 * layers1 + 2 * (l + 1)))
                pe.wait_ge(S["yp_ready"], c.next("yp_ready", 3))
                c.add(("frees", "yp_ready"), 2)
                for j in range(4):
                    project("dve", "resid", x2mv)
                layer_norm_sums()
                c.block = 1
                if l == LAYERS - 1:
                    route()
                    ffn(CHUNKS * EXPERTS)
                else:
                    ffn(CHUNKS)
                layer_norm_sums()

            def layer_norm_sums():
                pe.wait_ge(S["resid"], c.next("resid", 4))
                bank = unit("act", "std_ready")
                for k in range(KT):
                    last = mm(bank[:, 0:T], ones[:, 0:P], hT3[:, k, :], k == 0, k == KT - 1)
                last.then_inc(S["act_full"], 1)
                norm_sum()

            def route():
                pe.wait_ge(S["x2_ready"], c.at("x2_ready", c.get(("seen", "x2_ready")) + 1))
                bank = unit("dve", "top_logits")
                for tt in range(2):
                    for k in range(KT):
                        last = mm(bank[:, tt * 8:tt * 8 + 8], hT3[:, k, tt * P:(tt + 1) * P],
                                  prm("router", 0, 8 * k, 8), k == 0, k == KT - 1)
                last.then_inc(S["dve_full"], 1)
                pe.wait_ge(S["comb_ready"], c.next("comb_ready"))
                bank = unit("dve", "ct_ready")
                for tt in range(2):
                    last = pe.transpose(bank[0:8, tt * P:(tt + 1) * P], comb[:, tt * 8:tt * 8 + 8], c1("ident"))
                last.then_inc(S["dve_full"], 1)
                pe.wait_ge(S["ct_ready"], c.next("ct_ready"))
                for j in range(4):
                    bank = unit("dve", "cbc_ready")
                    for e in range(2):
                        last = mm(bank[:, e * T:(e + 1) * T], pick_row(8, 2 * j + e), Y[0:8, 0:T], True, True)
                    last.then_inc(S["dve_full"], 1)

            pe.wait_ge(S["setup_done"], c.at("setup_done", 1))
            pe.wait_ge(S["setup_in"], 48)
            for l in range(layers1):
                layer1(l)
            if layers2:
                pe.wait_ge(S["tab_in"], 16)
                c.add(("seen", "resid"), RESID_PER_LAYER * layers1)
            for l in range(layers2):
                c.block = 1
                layer2(l)

        @block.scalar
        def _(act):
            c = Count(act, n_slabs)
            go = nc.scalar.activation

            def slab():
                n = c.slab()
                for m in c.due():
                    r, d = m % RAW, m % SPLIT
                    act.wait_ge(S[f"slab_in{r}"], c.at(f"slab_in{r}", 16 * (m // RAW + 1)))
                    if m >= SPLIT:
                        act.wait_ge(S["slab_used"], c.at("slab_used", m - SPLIT + 1))
                    go(wh[:, d * SLAB:(d + 1) * SLAB], raw[:, r * SLAB:(r + 1) * SLAB],
                       ACT.Copy).then_inc(S["hi_done"], c.one("hi_done"))
                return n

            def bank_in(full=None):
                k = c.get("act_unit")
                c.add("act_unit")
                if full is None:
                    act.wait_ge(S["act_full"], c.next("act_full"))
                else:
                    act.wait_ge(S["slab_used"], c.at("slab_used", full + 1))
                return actb[:, k % 2, :]

            def stdbuf():
                k = c.add("std") - 1
                if k >= 2:
                    act.wait_ge(S["std_taken"], c.at("std_taken", k - 1))
                return std[:, (k % 2) * 512:(k % 2 + 1) * 512]

            def norm_std(scale=1.0 / D, e=0):
                s = stdbuf()
                go(s[:, 0:T], bank_in()[:, 0:T], ACT.Sqrt, bias=eps[:, e:e + 1], scale=scale).then_inc(S["std_ready"], c.one("std_ready"))

            def rms():
                go(U[:, :], hT[:, :], ACT.Square).then_inc(S["sq_ready"], c.one("sq_ready"))
                norm_std()

            def ffn(chunks):
                def step(k):
                    q = c.get("chunk")
                    c.add("chunk")
                    n = slab()
                    b = bank_in(n)
                    if k >= 2 or q >= 2:
                        act.wait_ge(S["h_mul"], c.at("h_mul", q - 1))
                    go(SIL[c.block][:, (q % 2) * 512:(q % 2 + 1) * 512], b, ACT.Silu).then_inc(S["sil_ready"], c.one("sil_ready"))
                    slab()
                    if k:
                        slab()
                step(0)
                step(1)
                with c.turns((chunks - 3) // 2, FFN_TURN):
                    step(2)
                    step(3)
                for k in range(2 + (chunks - 3) // 2 * 2, chunks):
                    step(k)
                slab()

            def std512(scale):
                s = stdbuf()
                go(s, bank_in(), ACT.Sqrt, bias=eps[:, 0:1], scale=scale).then_inc(S["std_ready"], c.one("std_ready"))

            def heads_in(dst, tokens=False):
                n = slab()
                b = bank_in(n)
                k = c.add("sqa") - 1
                go(dst, b, ACT.Copy)
                go(sqa[:, (k % 2) * 512:(k % 2 + 1) * 512], b, ACT.Square).then_inc(S["sqa_ready"], c.one("sqa_ready"))

            def layer1(l):
                if l == 0:
                    act.wait_ge(S["setup_done"], c.at("setup_done", 1))
                    act.wait_ge(S["setup_in"], 48)
                else:
                    act.wait_ge(S["resid"], c.next("resid", 4))
                rms()
                ffn(CHUNKS)
                act.wait_ge(S["resid"], c.next("resid", 4))
                rms()
                r = lambda k: rows8[0:4, k * T:(k + 1) * T]
                act.wait_ge(S["gate_abs"], c.next("gate_abs"))
                go(r(3), r(2), ACT.Exp, scale=-1.0).then_inc(S["act_step"], c.one("act_step"))
                act.wait_ge(S["act_step"], c.own("act_step"))
                go(r(4), r(3), ACT.Ln, bias=1.0).then_inc(S["gate_ln"], c.one("gate_ln"))
                for j in range(8):
                    slab()
                    if j >= 1:
                        act.wait_ge(S["conv_done"], c.next("conv_done"))
                        conv_out(j - 1)
                    if j == 3:
                        go(gcol, bank_in()[:, 0:8], ACT.Copy).then_inc(S["act_free"], c.one("act_free"))
                for j in range(4):
                    n = slab()
                    if j == 0:
                        act.wait_ge(S["conv_done"], c.next("conv_done"))
                        conv_out(7)
                    go(vtok[:, :, j * T:(j + 1) * T], bank_in(n).rearrange("p (s f) -> p s f", s=2), ACT.Copy).then_inc(S["act_free"], c.one("act_free"))
                for j in range(4):
                    heads_in(aq[:, j * 512:(j + 1) * 512])
                    if j:
                        std512(1.0 / HEAD)
                heads_in(ak)
                std512(1.0 / HEAD)
                go(av, bank_in(slab()), ACT.Copy).then_inc(S["act_free"], c.one("act_free"))
                std512(1.0 / HEAD)

                for i in range(M_HEADS + 2):
                    if 1 <= i <= M_HEADS:
                        h = i - 1
                        b = bank_in(slab())
                        if h >= 2:
                            act.wait_ge(S["hm_split"], c.at("hm_split", 4 * l + h - 1))
                        go(sigo[:, (h % 2) * 512:(h % 2 + 1) * 512], b, ACT.Sigmoid).then_inc(S["sigo_ready"], c.one("sigo_ready"))
                    if i < M_HEADS:
                        a = warg[:, (i % 2) * 640:(i % 2 + 1) * 640]
                        act.wait_ge(S["arg_ready"], c.next("arg_ready"))
                        go(a[:, 0:T], a[:, 0:T], ACT.Exp, bias=gcol[:, i:i + 1], scale=-1.0)
                        go(a[:, T:384], a[:, T:384], ACT.Exp, bias=gcol[:, 4 + i:5 + i], scale=-1.0)
                        go(a[:, 384:640], a[:, 384:640], ACT.Exp, scale=-1.0).then_inc(S["w_ready"], c.one("w_ready"))
                    if 1 <= i <= M_HEADS:
                        go(dn, bank_in()[:, 0:T], ACT.Abs).then_inc(S["den_ready"], c.one("den_ready"))
                    if i < M_HEADS:
                        go(sgm[:, i * 512:(i + 1) * 512], bank_in(slab()), ACT.Sigmoid).then_inc(S["sg_ready"], c.one("sg_ready"))
                    if 1 <= i <= M_HEADS:
                        b = (i - 1) % 2
                        act.wait_ge(S["hm_ready"], c.next("hm_ready"))
                        go(sqm[:, b * 512:(b + 1) * 512], hm[:, b * 512:(b + 1) * 512], ACT.Square).then_inc(S["sqm_ready"], c.one("sqm_ready"))
                    if i < M_HEADS:
                        go(sga[:, i * 512:(i + 1) * 512], bank_in(slab()), ACT.Sigmoid).then_inc(S["sg_ready"], c.one("sg_ready"))
                    if i >= 2:
                        norm_std(1.0 / T)
                items = [(g, b) for g in range(KV_HEADS) for b in range(2)]
                for i in range(len(items) + 2):
                    if i < 4:
                        slab()
                    if i < len(items):
                        nk = items[i][1] + 1
                        sc = SCB[c.block][:, (i % 2) * 1024:(i % 2) * 1024 + 4 * nk * P].rearrange("p (h k) -> p h k", h=4)
                        st = SMALL[c.block][:, (i % 2) * 32:(i % 2 + 1) * 32]
                        act.wait_ge(S["nmx_ready"], c.next("nmx_ready"))
                        for hh in range(4):
                            go(sc[:, hh, :], sc[:, hh, :], ACT.Exp, bias=st[:, 4 + hh:5 + hh],
                               accum_out=st[:, 12 + hh:13 + hh])
                        go(st[:, 16:20], st[:, 8:12], ACT.Exp).then_inc(S["exp_ready"], c.one("exp_ready"))
                    if 1 <= i <= len(items):
                        copy_probs(i - 1, items[i - 1][1] + 1)
                for j in range(8):
                    slab()
                act.wait_ge(S["resid"], c.next("resid", 4))
                act.dma_start(pf.rearrange("p (k t) -> p k t", k=2), p_t[l]).then_inc(S["p_in"], 16)
                rms()
                ffn(CHUNKS)
                act.wait_ge(S["resid"], c.next("resid", 4))
                rms()
                for j in range(4):
                    go(sgm[:, j * 512:(j + 1) * 512], bank_in(slab()), ACT.Sigmoid).then_inc(S["sg_ready"], c.one("sg_ready"))
                slab()

            def square(dst, src):
                go(dst, src, ACT.Square).then_inc(S["sq_ready"], c.one("sq_ready"))

            def layer2(l):
                for j in range(6):
                    slab()
                    if j == 1:
                        act.wait_ge(S["gate_abs"], c.next("gate_abs"))
                        go(rows2[0:4, 0:T], rows2b[0:4, 0:T], ACT.Sigmoid)
                        go(rows2[0:4, 3 * T:4 * T], rows2[0:4, 2 * T:3 * T], ACT.Exp, scale=-1.0).then_inc(S["act_step"], c.one("act_step"))
                        act.wait_ge(S["act_step"], c.own("act_step"))
                        go(rows2b[0:4, 4 * T - 1:4 * T], prm("b_a_log_2", l, rows=4), ACT.Exp)
                        go(rows2b[0:4, 2 * T:3 * T], rows2[0:4, 3 * T:4 * T], ACT.Ln, bias=1.0).then_inc(S["gate_ln"], c.one("gate_ln"))
                    if j >= 1:
                        act.wait_ge(S["conv_done"], c.next("conv_done"))
                        conv_out(j - 1)
                        if j - 1 < 4:
                            act.wait_ge(S["qk_ready"], c.own("qk_ready"))
                            square(U[:, (j - 1) * 512:j * 512], qkvc[:, (j - 1) * 512:j * 512])
                    if j >= 2:
                        s = stdbuf()
                        go(s, bank_in(), ACT.Sqrt, bias=eps[:, 0:1]).then_inc(S["std_ready"], c.one("std_ready"))
                    if j == 3:
                        go(col, bank_in()[:, 0:16], ACT.Copy).then_inc(S["col_ready"], c.one("col_ready"))
                act.wait_ge(S["conv_done"], c.next("conv_done"))
                conv_out(5)
                go(gtok, bank_in(slab()), ACT.Gelu_apprx_tanh).then_inc(S["gelu_ready"], c.one("gelu_ready"))
                act.wait_ge(S["ec_arg"], c.next("ec_arg"))
                go(sm2[:, 8:16], sm2[:, 0:8], ACT.Exp).then_inc(S["ec_ready"], c.one("ec_ready"))
                act.wait_ge(S["dt_arg"], c.next("dt_arg"))
                go(DT, DT, ACT.Exp).then_inc(S["dt_ready"], c.one("dt_ready"))
                for level in range(1, 7):
                    for ch in range(2):
                        go(Y[:, ch * 512:(ch + 1) * 512], bank_in(), ACT.Copy).then_inc(S["y_ready"], c.one("y_ready"))
                    n = slab()
                    if level == 2:
                        act.wait_ge(S["gv_arg"], c.next("gv_arg"))
                        go(small2[:, 4:6].unsqueeze(2), small2[:, 0:4].rearrange("p (s m) -> p s m", s=2)[:, :, 1:2],
                                  ACT.Sqrt, bias=eps[:, 1:2]).then_inc(S["gv_std"], c.one("gv_std"))
                    b = bank_in(n)
                    if level == 1:
                        go(utok, b, ACT.Gelu_apprx_tanh).then_inc(S["gelu_ready"], c.one("gelu_ready"))
                    elif level in (2, 3):
                        go(cqk[:, (level - 2) * 512:(level - 1) * 512], b, ACT.Copy).then_inc(S["cqk_ready"], c.one("cqk_ready"))
                    elif level == 4:
                        go(cv, b, ACT.Copy).then_inc(S["cqk_ready"], c.one("cqk_ready"))
                    else:
                        go(silz[:, (level - 5) * 512:(level - 4) * 512], b, ACT.Silu).then_inc(S["silz_ready"], c.one("silz_ready"))
                act.wait_ge(S["qd_arg"], c.next("qd_arg"))
                go(QD, QD, ACT.Exp).then_inc(S["qd_exp"], c.one("qd_exp"))
                if l + 1 < layers2:
                    act.wait_ge(S["ya_ready"], c.at("ya_ready", l + 1))
                    act.dma_start(gmw, gmlp_w[l + 1]).then_inc(S["gmlp_in"], 16)
                go(WT, bank_in(), ACT.Copy).then_inc(S["wt_ready"], c.one("wt_ready"))
                go(St, bank_in(), ACT.Copy).then_inc(S["st_ready"], c.one("st_ready"))
                act.wait_ge(S["o_ready"], c.next("o_ready", 2))
                square(sqo, OT)
                for j in range(2):
                    s = stdbuf()
                    go(s, bank_in(), ACT.Sqrt, bias=eps[:, 0:1], scale=1.0 / P).then_inc(S["std_ready"], c.one("std_ready"))
                for i in range(2 + 2):
                    if i < 2:
                        nk = i + 1
                        sc = scb2[:, i * 1024:i * 1024 + 4 * nk * P].rearrange("p (h k) -> p h k", h=4)
                        st = small2[:, (i % 2) * 32:(i % 2 + 1) * 32]
                        act.wait_ge(S["nmx_ready"], c.next("nmx_ready"))
                        for hh in range(4):
                            last = go(sc[:, hh, :], sc[:, hh, :], ACT.Exp, bias=st[:, 4 + hh:5 + hh])
                        last.then_inc(S["exp_ready"], c.one("exp_ready"))
                    if 1 <= i <= 2:
                        copy_probs(i - 1, i)
                for j in range(4):
                    slab()
                layer_norm()
                if l == LAYERS - 1:
                    act.wait_ge(S["top_arg"], c.next("top_arg"))
                    go(comb[:, 32:34], comb[:, 34:36], ACT.Exp).then_inc(S["top_exp"], c.one("top_exp"))
                    ffn(CHUNKS * EXPERTS)
                else:
                    ffn(CHUNKS)
                layer_norm()

            def layer_norm():
                s = stdbuf()
                go(s[:, 0:T], bank_in()[:, 0:T], ACT.Copy, scale=1.0 / D).then_inc(S["std_ready"], c.one("std_ready"))
                act.wait_ge(S["std_taken"], c.at("std_taken", c.get("std")))
                square(U[:, :], hT[:, :])
                norm_std(e=1)

            def conv_out(j):
                go(QKC[c.block][:, j * 512:(j + 1) * 512], CACC[c.block][:, (j % 2) * 512:(j % 2 + 1) * 512], ACT.Silu).then_inc(S["qk_ready"], c.one("qk_ready"))

            def copy_probs(i, nk):
                for kb in range(nk):
                    o = (i % 2) * 1024 + kb * 512
                    go(PTB[c.block][:, o:o + 512], bank_in(), ACT.Copy).then_inc(S["pt_ready"], c.one("pt_ready"))

            for l in range(layers1):
                layer1(l)
            if layers2:
                if layers1:
                    act.wait_ge(S["resid"], c.next("resid", 4))
                else:
                    act.wait_ge(S["setup_done"], c.at("setup_done", 1))
                    act.wait_ge(S["setup_in"], 48)
                act.dma_start(tab, const2).then_inc(S["tab_in"], 16)
                act.dma_start(gmw, gmlp_w[0]).then_inc(S["gmlp_in"], 16)
                act.wait_ge(S["tab_in"], 16)
                act.wait_ge(S["gmlp_in"], 16)
            for l in range(layers2):
                c.block = 1
                layer2(l)

        @block.vector
        def _(dve):
            c = Count(dve, n_slabs)
            V = nc.vector
            TT, STT, TS = V.tensor_tensor, V.scalar_tensor_tensor, V.tensor_scalar

            def slab():
                n = c.slab()
                for m in c.due():
                    r, d = m % RAW * SLAB, m % SPLIT * SLAB
                    dve.wait_ge(S["hi_done"], c.at("hi_done", m + 1))
                    TT(wl[:, d:d + HALF], raw[:, r:r + HALF], asf(wh[:, d:d + HALF]),
                       ALU.subtract).then_inc(S["lo_dve"], c.one("lo_dve"))
                return n

            def bank_in(full=None):
                k = c.get("dve_unit")
                c.add("dve_unit")
                if full is None:
                    dve.wait_ge(S["dve_full"], c.next("dve_full"))
                else:
                    dve.wait_ge(S["slab_used"], c.at("slab_used", full + 1))
                return dveb[:, k % 2, :]

            def stdbuf():
                k = c.add("std") - 1
                return std[:, (k % 2) * 512:(k % 2 + 1) * 512]

            def split(dst, src, done, which=slice(None)):
                hi, lo = dst
                V.tensor_copy(hi, src).then_inc(S["dve_step"], c.one("dve_step"))
                dve.wait_ge(S["dve_step"], c.own("dve_step"))
                TT(lo, src, asf(hi), ALU.subtract).then_inc(S[done], c.one(done))

            def rms(gain, l):
                dve.wait_ge(S["std_ready"], c.next("std_ready"))
                s = stdbuf()
                if c.get(("made", "x2_ready")):
                    dve.wait_ge(S["x2_ready"], c.own("x2_ready"))
                V.reciprocal(rinv[:, 0:T], s[:, 0:T]).then_inc(S["std_taken"], c.one("std_taken"))
                dve.wait_ge(S["std_taken"], c.own("std_taken"))
                for k in range(KT):
                    last = STT(U3[:, k, :], hT3[:, k, :], prm(gain, l, k), rinv[:, 0:T], ALU.mult, ALU.mult)
                last.then_inc(S["dve_step"], c.one("dve_step"))
                dve.wait_ge(S["dve_step"], c.own("dve_step"))
                split((x2v[:, 0], x2v[:, 1]), U3, "x2_ready")

            def ffn(chunks, routed=False):
                def step(k):
                    q = c.get("chunk")
                    c.add("chunk")
                    slab()
                    n = slab()
                    b = bank_in(n)
                    dve.wait_ge(S["sil_ready"], c.next("sil_ready"))
                    o = (q % 2) * 512
                    TT(HF[c.block][:, o:o + 512], SIL[c.block][:, o:o + 512], b, ALU.mult).then_inc(S["h_mul"], c.one("h_mul"))
                    dve.wait_ge(S["h_mul"], c.own("h_mul"))
                    h3 = HF[c.block][:, o:o + 512].rearrange("p (k t) -> p k t", k=2)
                    if routed:
                        e = k // CHUNKS if c.i is None else (c.i * 2 + k) // CHUNKS
                        TT(h3, h3, cbc[:, bass.ds(e * T, T)].unsqueeze(1).to_broadcast([P, 2, T]), ALU.mult).then_inc(S["dve_step"], c.one("dve_step"))
                        dve.wait_ge(S["dve_step"], c.own("dve_step"))
                    split((h2v[:, q % 2, 0], h2v[:, q % 2, 1]), h3, "h_ready")
                    if k:
                        slab()
                step(0)
                step(1)
                with c.turns((chunks - 3) // 2, {**FFN_TURN, "dve_step": 4 if routed else 2}):
                    step(2)
                    step(3)
                for k in range(2 + (chunks - 3) // 2 * 2, chunks):
                    step(k)
                n = slab()
                dve.wait_ge(S["slab_used"], c.at("slab_used", n + 1))

            def add_ffn(scale):
                for j in range(4):
                    o = j * 512
                    STT(hT[:, o:o + 512], acc[:, j, :], scale, hT[:, o:o + 512], ALU.mult, ALU.add).then_inc(S["resid"], c.one("resid"))

            def conv(j, name, l, tile_count, bias=None):
                n = slab()
                b = bank_in(n)
                if c.get("convs") >= 2:
                    dve.wait_ge(S["qk_ready"], c.at("qk_ready", c.get("convs") - 1))
                c.add("convs")
                y = CACC[c.block][:, (j % 2) * 512:(j % 2 + 1) * 512]
                for t in range(2):
                    k = 2 * j + t
                    args = (prm(bias, l, k), ALU.mult, ALU.add) if bias else (None, ALU.mult)
                    last = TS(y[:, t * T:(t + 1) * T], b[:, t * T:(t + 1) * T], prm(name, l, 3 * tile_count + k), *args)
                last.then_inc(S["dve_step"], c.one("dve_step"))
                dve.wait_ge(S["dve_step"], c.own("dve_step"))
                for s in range(1, 4):
                    for t in range(2):
                        k = 2 * j + t
                        yy = y[:, t * T + s:(t + 1) * T]
                        last = STT(yy, b[:, t * T:(t + 1) * T - s], prm(name, l, (3 - s) * tile_count + k), yy,
                                   ALU.mult, ALU.add)
                    if s < 3:
                        last.then_inc(S["dve_step"], c.one("dve_step"))
                        dve.wait_ge(S["dve_step"], c.own("dve_step"))
                last.then_inc(S["conv_done"], c.one("conv_done"))

            def norm_heads(dst, name, l):
                dve.wait_ge(S["std_ready"], c.next("std_ready"))
                s = stdbuf()
                if c.get(("made", "an_ready")):
                    dve.wait_ge(S["an_ready"], c.own("an_ready"))
                V.reciprocal(rinv, s).then_inc(S["std_taken"], c.one("std_taken"))
                dve.wait_ge(S["std_taken"], c.own("std_taken"))
                STT(dst, dst, prm(name, l), rinv, ALU.mult, ALU.mult).then_inc(S["an_ready"], c.one("an_ready"))

            def layer1(l):
                if l == 0:
                    dve.wait_ge(S["setup_done"], c.at("setup_done", 1))
                    dve.wait_ge(S["setup_in"], 48)
                rms("ffn1_norm", l)
                ffn(CHUNKS)
                add_ffn(0.5)
                rms("mix_norm", l)
                r = lambda k: rows8[0:4, k * T:(k + 1) * T]
                fx, ig, ab, ln, lf, F, g = (r(k) for k in (0, 1, 2, 4, 5, 6, 7))
                b = bank_in()
                TS(fx, b[0:4, T:2 * T], prm("m_fgate_b", l, rows=4), None, ALU.add)
                TS(ig, b[0:4, 0:T], prm("m_igate_b", l, rows=4), None, ALU.add).then_inc(S["dve_free"], c.one("dve_free"))
                dve.wait_ge(S["dve_free"], c.own("dve_free"))
                STT(ab, fx, -1.0, fx, ALU.mult, ALU.max).then_inc(S["gate_abs"], c.one("gate_abs"))
                dve.wait_ge(S["gate_ln"], c.next("gate_ln"))
                STT(lf, fx, 0.0, ln, ALU.min, ALU.subtract).then_inc(S["dve_step"], c.one("dve_step"))
                dve.wait_ge(S["dve_step"], c.own("dve_step"))
                V.tensor_tensor_scan(F, ones[0:4, :], lf, 0.0, ALU.mult, ALU.add).then_inc(S["dve_step"], c.one("dve_step"))
                dve.wait_ge(S["dve_step"], c.own("dve_step"))
                TT(g, ig, F, ALU.subtract).then_inc(S["dve_step"], c.one("dve_step"))
                dve.wait_ge(S["dve_step"], c.own("dve_step"))
                M, m = MM[0:4, 0:T], MM[0:4, T:2 * T]
                V.tensor_tensor_scan(M, g, g, 0.0, ALU.max, ALU.max).then_inc(S["dve_step"], c.one("dve_step"))
                dve.wait_ge(S["dve_step"], c.own("dve_step"))
                TT(m, M, F, ALU.add).then_inc(S["rows_ready"], c.one("rows_ready"))
                for j in range(8):
                    conv(j, "m_conv_w", l, 16, "m_conv_b")
                for j in range(4):
                    slab()
                for j in range(4):
                    slab()
                    if j:
                        norm_heads(aq[:, (j - 1) * 512:j * 512], "a_q_norm", l)
                slab()
                norm_heads(aq[:, 3 * 512:4 * 512], "a_q_norm", l)
                slab()
                norm_heads(ak, "a_k_norm", l)
                V.tensor_copy(aks, bank_in()).then_inc(S["dve_free"], c.one("dve_free"))

                tri = c1("tri")
                for i in range(M_HEADS + 2):
                    if 1 <= i <= M_HEADS:
                        slab()
                    if i < M_HEADS:
                        a = warg[:, (i % 2) * 640:(i % 2 + 1) * 640]
                        b = bank_in()
                        if c.get(("made", "s_ready")):
                            dve.wait_ge(S["s_ready"], c.own("s_ready"))
                        TT(a[:, 0:P], b[:, 0:P], tri, ALU.add)
                        V.tensor_copy(a[:, P:T], b[:, P:T])
                        TT(a[:, T:384], b[:, P:T], tri, ALU.add)
                        V.tensor_copy(a[:, 384:640], b[:, T:2 * T]).then_inc(S["arg_ready"], c.one("arg_ready"))
                    if 1 <= i <= M_HEADS:
                        q = (i - 1) % 2
                        b = bank_in()
                        dve.wait_ge(S["den_ready"], c.next("den_ready"))
                        if c.get(("made", "hm_split")):
                            dve.wait_ge(S["hm_split"], c.own("hm_split"))
                        TT(dn, dn, warg[:, q * 640 + 384:q * 640 + 640], ALU.max).then_inc(S["dve_step"], c.one("dve_step"))
                        dve.wait_ge(S["dve_step"], c.own("dve_step"))
                        V.reciprocal(dn, dn).then_inc(S["dve_step"], c.one("dve_step"))
                        dve.wait_ge(S["dve_step"], c.own("dve_step"))
                        TT(hm[:, q * 512:(q + 1) * 512].rearrange("p (v t) -> p v t", v=2),
                                  b.rearrange("p (v t) -> p v t", v=2),
                                  dn.unsqueeze(1).to_broadcast([P, 2, T]), ALU.mult).then_inc(S["hm_ready"], c.one("hm_ready"))
                    if i < M_HEADS:
                        slab()
                        b = bank_in()
                        dve.wait_ge(S["w_ready"], c.next("w_ready"))
                        q = i % 2
                        STT(Sw[:, q * 384:(q + 1) * 384], b[:, 0:384], 1.0 / 16.0,
                                   warg[:, q * 640:q * 640 + 384], ALU.mult, ALU.mult).then_inc(S["s_ready"], c.one("s_ready"))
                        slab()
                    if i >= 2:
                        h, q = i - 2, i % 2
                        dve.wait_ge(S["std_ready"], c.next("std_ready"))
                        dve.wait_ge(S["sigo_ready"], c.next("sigo_ready"))
                        s = stdbuf()
                        V.reciprocal(rinv[:, 0:T], s[:, 0:T]).then_inc(S["std_taken"], c.one("std_taken"))
                        dve.wait_ge(S["std_taken"], c.own("std_taken"))
                        hh = hm[:, q * 512:(q + 1) * 512]
                        for vt in range(2):
                            last = STT(hh[:, vt * T:(vt + 1) * T], hh[:, vt * T:(vt + 1) * T],
                                       prm("m_out_norm", l, 2 * h + vt), rinv[:, 0:T], ALU.mult, ALU.mult)
                        last.then_inc(S["dve_step"], c.one("dve_step"))
                        dve.wait_ge(S["dve_step"], c.own("dve_step"))
                        TT(hh, hh, sigo[:, q * 512:(q + 1) * 512], ALU.mult).then_inc(S["dve_step"], c.one("dve_step"))
                        dve.wait_ge(S["dve_step"], c.own("dve_step"))
                        split((x2mv[:, 0, 2 * h:2 * h + 2, :], x2mv[:, 1, 2 * h:2 * h + 2, :]),
                              hh.rearrange("p (v t) -> p v t", v=2), "hm_split")
                items = [(g, b) for g in range(KV_HEADS) for b in range(2)]
                for i in range(len(items) + 2):
                    if i < 4:
                        if i == 0:
                            dve.wait_ge(S["sg_ready"], c.next("sg_ready", 8))
                        b = bank_in(slab())
                        s = sgm[:, i * 512:(i + 1) * 512]
                        TT(s, s, b, ALU.mult).then_inc(S["gated"], c.one("gated"))
                    if i < len(items):
                        g, b = items[i]
                        scores_in(i, b, c1("up") if b == 0 else c1("anti", width=2 * P),
                                  prm("a_sinks", l, 4 * g, 4))
                    if i >= 2:
                        g, b = items[i - 2]
                        heads_out(x2v, 2 * g, b)
                    if i < len(items):
                        probs_out(i, items[i][1] + 1, True)
                for j in range(4):
                    b = bank_in(slab())
                    t = tmp
                    TT(t, sga[:, j * 512:(j + 1) * 512], b, ALU.mult).then_inc(S["gated"], c.one("gated"))
                    dve.wait_ge(S["gated"], c.own("gated"))
                    TT(t, t, sgm[:, j * 512:(j + 1) * 512], ALU.add).then_inc(S["dve_step"], c.one("dve_step"))
                    dve.wait_ge(S["dve_step"], c.own("dve_step"))
                    split((x2mv[:, 0, 2 * j:2 * j + 2, :], x2mv[:, 1, 2 * j:2 * j + 2, :]),
                          t.rearrange("p (v t) -> p v t", v=2), "x2m_ready")
                    dve.wait_ge(S["x2m_ready"], c.own("x2m_ready"))
                for j in range(4):
                    b = bank_in(slab())
                    h = hT[:, j * 512:(j + 1) * 512]
                    TT(h, h, b, ALU.add).then_inc(S["resid"], c.one("resid"))
                dve.wait_ge(S["resid"], c.own("resid"))
                rms("ffn2_norm", l)
                ffn(CHUNKS)
                add_ffn(0.5)
                rms("ple_norm", l)
                dve.wait_ge(S["p_in"], 16 * (l + 1))
                dve.wait_ge(S["slab_used"], c.at("slab_used", c.get("slab")))
                split((h2v[:, 0, 0], h2v[:, 0, 1]), pf.rearrange("p (k t) -> p k t", k=2), "psplit_ready")
                for j in range(4):
                    slab()
                n = slab()
                dve.wait_ge(S["sg_ready"], c.next("sg_ready", 4))
                for j in range(4):
                    b = bank_in(None if j < 3 else n)
                    TT(tmp, sgm[:, j * 512:(j + 1) * 512], b, ALU.mult).then_inc(S["gated"], c.one("gated"))
                    dve.wait_ge(S["gated"], c.own("gated"))
                    h = hT[:, j * 512:(j + 1) * 512]
                    TT(h, h, tmp, ALU.add).then_inc(S["resid"], c.one("resid"))
                    dve.wait_ge(S["resid"], c.own("resid"))

            def scores_in(i, b, mask, sinks):
                nk = b + 1
                sc = SCB[c.block][:, (i % 2) * 1024:(i % 2) * 1024 + 4 * nk * P].rearrange("p (h k) -> p h k", h=4)
                st = SMALL[c.block][:, (i % 2) * 32:(i % 2 + 1) * 32]
                for half in range(2):
                    bb = bank_in()[:, 0:2 * nk * P].rearrange("p (h k) -> p h k", h=2)
                    STT(sc[:, half::2, :], bb, 0.125,
                               mask.unsqueeze(1).to_broadcast([P, 2, nk * P]), ALU.mult, ALU.add).then_inc(S["sc_masked"], c.one("sc_masked"))
                dve.wait_ge(S["sc_masked"], c.own("sc_masked"))
                V.tensor_reduce(st[:, 0:4], sc, AX.X, ALU.max).then_inc(S["dve_step"], c.one("dve_step"))
                dve.wait_ge(S["dve_step"], c.own("dve_step"))
                if sinks is not None:
                    TT(st[:, 0:4], st[:, 0:4], sinks, ALU.max).then_inc(S["dve_step"], c.one("dve_step"))
                    dve.wait_ge(S["dve_step"], c.own("dve_step"))
                    TS(st[:, 4:8], st[:, 0:4], -1.0, None, ALU.mult).then_inc(S["dve_step"], c.one("dve_step"))
                    dve.wait_ge(S["dve_step"], c.own("dve_step"))
                    TT(st[:, 8:12], sinks, st[:, 4:8], ALU.add).then_inc(S["nmx_ready"], c.one("nmx_ready"))
                else:
                    TS(st[:, 4:8], st[:, 0:4], -1.0, None, ALU.mult).then_inc(S["nmx_ready"], c.one("nmx_ready"))

            def probs_out(i, nk, sinks, count=None):
                sc = SCB[c.block][:, (i % 2) * 1024:(i % 2) * 1024 + 4 * nk * P].rearrange("p (h k) -> p h k", h=4)
                st = SMALL[c.block][:, (i % 2) * 32:(i % 2 + 1) * 32]
                dve.wait_ge(S["exp_ready"], c.next("exp_ready"))
                if sinks:
                    TT(st[:, 12:16], st[:, 12:16], st[:, 16:20], ALU.add).then_inc(S["dve_step"], c.one("dve_step"))
                    dve.wait_ge(S["dve_step"], c.own("dve_step"))
                else:
                    TT(sc, sc, count.unsqueeze(1).to_broadcast([P, 4, nk * P]), ALU.mult).then_inc(S["dve_step"], c.one("dve_step"))
                    dve.wait_ge(S["dve_step"], c.own("dve_step"))
                    V.tensor_reduce(st[:, 12:16], sc, AX.X, ALU.add).then_inc(S["dve_step"], c.one("dve_step"))
                    dve.wait_ge(S["dve_step"], c.own("dve_step"))
                V.reciprocal(st[:, 20:24], st[:, 12:16]).then_inc(S["dve_step"], c.one("dve_step"))
                dve.wait_ge(S["dve_step"], c.own("dve_step"))
                TT(sc, sc, st[:, 20:24].unsqueeze(2).to_broadcast([P, 4, nk * P]), ALU.mult).then_inc(S["p_ready"], c.one("p_ready"))

            def heads_out(dst, tile, b):
                bb = bank_in()[:, 0:2 * P].rearrange("p (k t) -> p k t", k=2)
                o = slice(b * P, (b + 1) * P)
                split((dst[:, 0, tile:tile + 2, o], dst[:, 1, tile:tile + 2, o]), bb, "ha_ready")

            def bc4(t, n=P):
                return t.unsqueeze(1).to_broadcast([P, 4, n])

            def each4(t, n=P):
                return t.unsqueeze(2).to_broadcast([P, 4, n])

            def layer2(l):
                split((x2v[:, 0], x2v[:, 1]), hT3, "x2_ready")
                b = bank_in()
                bx, ax, ab, ln, g = rows2b[0:4, 0:T], rows2b[0:4, T:2 * T], rows2[0:4, 2 * T:3 * T], \
                    rows2b[0:4, 2 * T:3 * T], rows2b[0:4, 3 * T:4 * T - 1]
                gx = rows2[0:4, 2 * T:3 * T]
                ea = rows2b[0:4, 4 * T - 1:4 * T]
                V.tensor_copy(bx, b[0:4, 0:T])
                TS(ax, b[0:4, T:2 * T], prm("b_dt_bias_2", l, rows=4), None, ALU.add).then_inc(S["dve_free"], c.one("dve_free"))
                dve.wait_ge(S["dve_free"], c.own("dve_free"))
                STT(ab, ax, -1.0, ax, ALU.mult, ALU.max).then_inc(S["gate_abs"], c.one("gate_abs"))
                conv(0, "conv_w_2", l, 12)
                conv(1, "conv_w_2", l, 12)
                dve.wait_ge(S["gate_ln"], c.next("gate_ln"))
                STT(gx, ax, 0.0, ln, ALU.max, ALU.add).then_inc(S["dve_step"], c.one("dve_step"))
                dve.wait_ge(S["dve_step"], c.own("dve_step"))
                TS(gx, gx, ea, -1.0, ALU.mult, ALU.mult).then_inc(S["dve_step"], c.one("dve_step"))
                dve.wait_ge(S["dve_step"], c.own("dve_step"))
                for ch in range(2):
                    last = V.tensor_tensor_scan(rows2[0:4, T + ch * P:T + (ch + 1) * P], ones[0:4, 0:P],
                                                gx[:, ch * P:(ch + 1) * P], 0.0, ALU.mult, ALU.add)
                last.then_inc(S["rows_ready"], c.one("rows_ready"))

                def norm_qk(j):
                    dve.wait_ge(S["std_ready"], c.next("std_ready"))
                    s = stdbuf()
                    if c.get(("made", "an_ready")):
                        dve.wait_ge(S["an_ready"], c.own("an_ready"))
                    V.reciprocal(rinv2, s).then_inc(S["std_taken"], c.one("std_taken"))
                    dve.wait_ge(S["std_taken"], c.own("std_taken"))
                    d = qkvc[:, j * 512:(j + 1) * 512]
                    STT(d, d, float(P ** -0.5) if j < 2 else 1.0, rinv2, ALU.mult, ALU.mult).then_inc(S["an_ready"], c.one("an_ready"))
                for j in range(2, 6):
                    conv(j, "conv_w_2", l, 12)
                    if j == 2:
                        dve.wait_ge(S["qk_ready"], c.at("qk_ready", c.get("convs") - 1))
                    norm_qk(j - 2)
                    if j == 3:
                        for h in range(4):
                            V.tensor_copy(BC[:, h * 512:(h + 1) * 512], bank_in()).then_inc(S["bc_ready"], c.one("bc_ready"))
                slab()
                dve.wait_ge(S["bc_ready"], c.own("bc_ready"))
                dve.wait_ge(S["col_ready"], c.next("col_ready"))
                BC4 = BC.rearrange("p (h w t) -> p h w t", h=4, w=2)
                colv = lambda ch, part: col[:, (2 * ch + part) * 4:(2 * ch + part + 1) * 4]
                TT(sm2[:, 0:4], BC4[:, :, 1, P - 1], colv(0, 1), ALU.subtract)
                V.tensor_copy(sm2[:, 4:8], colv(1, 1)).then_inc(S["ec_arg"], c.one("ec_arg"))
                for ch in range(2):
                    for h in range(4):
                        o = (4 * ch + h) * P
                        last = STT(DT[:, o:o + P], BC4[:, h, 1, ch * P:(ch + 1) * P], colv(ch, 1)[:, h:h + 1],
                                   c1("tri"), ALU.subtract, ALU.subtract)
                last.then_inc(S["dt_arg"], c.one("dt_arg"))
                dve.wait_ge(S["ec_ready"], c.next("ec_ready"))
                TT(sm2[:, 16:20], sm2[:, 12:16], colv(1, 0), ALU.mult).then_inc(S["dve_step"], c.one("dve_step"))
                dve.wait_ge(S["dve_step"], c.own("dve_step"))
                dve.wait_ge(S["dt_ready"], c.next("dt_ready"))
                c8 = lambda t, ch: t[:, ch * 512:(ch + 1) * 512]
                for ch in range(2):
                    TT(c8(MT, ch), c8(DT, ch), bank_in(), ALU.mult).then_inc(S["g_ready"], c.one("g_ready"))
                    dve.wait_ge(S["g_ready"], c.own("g_ready"))
                    TT(g4(c8(MT, ch)), g4(c8(MT, ch)), BC4[:, :, 0, ch * P:(ch + 1) * P], ALU.mult).then_inc(S["dve_step"], c.one("dve_step"))
                    dve.wait_ge(S["dve_step"], c.own("dve_step"))
                    TT(c8(AT, ch), c8(DT, ch), bank_in(), ALU.mult).then_inc(S["g_ready"], c.one("g_ready"))
                for ch in range(2):
                    TT(g4(c8(X, ch)), g4(c8(MT, ch)), bc4(t2("level", 0, P)), ALU.mult).then_inc(S["dve_step"], c.one("dve_step"))
                    dve.wait_ge(S["dve_step"], c.own("dve_step"))
                    TT(g4(c8(XT, ch)), bc4(c1("ident")), g4(c8(X, ch)), ALU.subtract).then_inc(S["xt_ready"], c.one("xt_ready"))
                dve.wait_ge(S["xt_ready"], c.own("xt_ready"))
                for ch in range(2):
                    V.tensor_copy(c8(X, ch), bank_in()).then_inc(S["x_new"], c.one("x_new"))
                for level in range(1, 7):
                    dve.wait_ge(S["x_new"], c.own("x_new"))
                    for ch in range(2):
                        TT(g4(c8(MLT, ch)), g4(c8(MT, ch)), bc4(t2("level", level * P, P)), ALU.mult).then_inc(S["ml_ready"], c.one("ml_ready"))
                    slab()
                    if level == 2:
                        dve.wait_ge(S["gelu_ready"], c.next("gelu_ready", 2))
                        norm_gmlp(l)
                    if level == 4:
                        u2 = utok.rearrange("p (s g d) -> p s g d", s=2, g=4)
                        b2 = bank_in().rearrange("p (s g d) -> p s g d", s=2, g=4)
                        for tt in range(2):
                            last = TT(gtok.rearrange("p (s g d) -> p s g d", s=2, g=4)[:, tt], b2[:, tt],
                                      prm("a_bs_2", l, 0, 4).unsqueeze(2).to_broadcast([P, 4, HEAD]), ALU.add)
                        last.then_inc(S["dve_step"], c.one("dve_step"))
                        dve.wait_ge(S["dve_step"], c.own("dve_step"))
                        TT(utok, utok, gtok, ALU.mult).then_inc(S["ya_ready"], c.one("ya_ready"))
                    if level == 5:
                        split((x2mv[:, 0, 0:2, :], x2mv[:, 1, 0:2, :]),
                              bank_in().rearrange("p (k t) -> p k t", k=2), "yp_ready")
                    if level == 6:
                        dve.wait_ge(S["cqk_ready"], c.next("cqk_ready", 3))
                        for j in range(2):
                            d = cqk[:, j * 512:(j + 1) * 512].rearrange("p (k t) -> p k t", k=2)
                            tb = gtok.rearrange("p (k t) -> p k t", k=2)
                            bb = bank_in().rearrange("p (k t) -> p k t", k=2)
                            two = lambda t: t.unsqueeze(1).to_broadcast([P, 2, T])
                            if c.get(("made", "rope_ready")):
                                dve.wait_ge(S["rope_ready"], c.own("rope_ready"))
                            TT(d, d, two(t2("cos")), ALU.mult).then_inc(S["dve_step"], c.one("dve_step"))
                            dve.wait_ge(S["dve_step"], c.own("dve_step"))
                            TT(tb, bb, two(t2("sin")), ALU.mult).then_inc(S["dve_step"], c.one("dve_step"))
                            dve.wait_ge(S["dve_step"], c.own("dve_step"))
                            TT(d, d, tb, ALU.add).then_inc(S["rope_ready"], c.one("rope_ready"))
                    for ch in range(2):
                        if level < 6:
                            TT(c8(X, ch), c8(X, ch), bank_in(), ALU.subtract).then_inc(S["x_new"], c.one("x_new"))
                        TT(c8(XT, ch), c8(XT, ch), bank_in(), ALU.subtract).then_inc(S["x_new"], c.one("x_new"))
                V.tensor_copy(g4(QD), BC4[:, :, 1, P:T]).then_inc(S["qd_arg"], c.one("qd_arg"))
                for ch in range(2):
                    TT(g4(c8(RV, ch)), g4(bank_in()), each4(colv(ch, 0)), ALU.mult).then_inc(S["rv_ready"], c.one("rv_ready"))
                TT(g4(KD), g4(bank_in()), each4(sm2[:, 8:12]), ALU.mult).then_inc(S["rv_ready"], c.one("rv_ready"))
                TT(g4(RK), g4(bank_in()), each4(sm2[:, 16:20]), ALU.mult).then_inc(S["rv_ready"], c.one("rv_ready"))
                dve.wait_ge(S["qd_exp"], c.next("qd_exp"))
                q1 = qkvc[:, 0:4 * T].rearrange("p (h t) -> p h t", h=4)[:, :, P:T]
                TT(g4(QD), g4(QD), q1, ALU.mult).then_inc(S["qd_ready"], c.one("qd_ready"))
                for ch in range(2):
                    V.tensor_copy(c8(Uc, ch), bank_in()).then_inc(S["u_ready"], c.one("u_ready"))
                OT4 = OT.rearrange("p (h t) -> p h t", h=4)
                V.tensor_copy(OT4[:, :, 0:P], g4(bank_in())).then_inc(S["o_ready"], c.one("o_ready"))
                dve.wait_ge(S["u_ready"], c.own("u_ready"))
                TT(VN, c8(Uc, 1), bank_in(), ALU.subtract).then_inc(S["vn_ready"], c.one("vn_ready"))
                V.tensor_copy(OT4[:, :, P:T], g4(bank_in())).then_inc(S["o_ready"], c.one("o_ready"))
                dve.wait_ge(S["o_ready"], c.own("o_ready"))
                dve.wait_ge(S["silz_ready"], c.next("silz_ready", 2))
                for j in range(2):
                    dve.wait_ge(S["std_ready"], c.next("std_ready"))
                    s = stdbuf()
                    V.reciprocal(rinv2, s).then_inc(S["std_taken"], c.one("std_taken"))
                    dve.wait_ge(S["std_taken"], c.own("std_taken"))
                    o = OT[:, j * 512:(j + 1) * 512]
                    STT(o, o, prm("b_norm_g_2", l), rinv2, ALU.mult, ALU.mult).then_inc(S["dve_step"], c.one("dve_step"))
                    dve.wait_ge(S["dve_step"], c.own("dve_step"))
                    TT(o, o, silz[:, j * 512:(j + 1) * 512], ALU.mult).then_inc(S["dve_step"], c.one("dve_step"))
                    dve.wait_ge(S["dve_step"], c.own("dve_step"))
                    split((x2mv[:, 0, 2 + 2 * j:4 + 2 * j, :], x2mv[:, 1, 2 + 2 * j:4 + 2 * j, :]),
                          o.rearrange("p (k t) -> p k t", k=2), "yp_ready")
                for i in range(2 + 2):
                    if i < 2:
                        scores_in(i, i, t2("dmask", 0, P) if i == 0 else t2("dmask", P, 2 * P), None)
                    if i >= 2:
                        heads_out(x2mv, 6, i - 2)
                    if i < 2:
                        probs_out(i, i + 1, False, t2("dcount", 0, P) if i == 0 else t2("dcount", P, 2 * P))
                for j in range(4):
                    b = bank_in(slab())
                    h = hT[:, j * 512:(j + 1) * 512]
                    STT(h, h, ALPHA, b, ALU.mult, ALU.add).then_inc(S["resid"], c.one("resid"))
                dve.wait_ge(S["resid"], c.own("resid"))
                layer_norm("ln1_g_2", "ln1_b_2", l)
                split((x2v[:, 0], x2v[:, 1]), hT3, "x2_ready")
                if l == LAYERS - 1:
                    route()
                    ffn(CHUNKS * EXPERTS, True)
                else:
                    ffn(CHUNKS)
                for j in range(4):
                    h = hT[:, j * 512:(j + 1) * 512]
                    STT(h, h, ALPHA, acc[:, j, :], ALU.mult, ALU.add).then_inc(S["resid"], c.one("resid"))
                dve.wait_ge(S["resid"], c.own("resid"))
                layer_norm("ln2_g_2", "ln2_b_2", l)

            def norm_gmlp(l):
                g2 = gtok.rearrange("p (s f) -> p s f", s=2)
                st = sm2[:, 20:32]
                for tt in range(2):
                    last = V.bn_stats(st[:, tt * 6:tt * 6 + 6], g2[:, tt, :])
                last.then_inc(S["dve_step"], c.one("dve_step"))
                dve.wait_ge(S["dve_step"], c.own("dve_step"))
                mv = small2[:, 0:4]
                for tt in range(2):
                    last = V.bn_aggr(mv[:, tt * 2:tt * 2 + 2], st[:, tt * 6:tt * 6 + 6])
                last.then_inc(S["gv_arg"], c.one("gv_arg"))
                dve.wait_ge(S["gv_arg"], c.own("gv_arg"))
                dve.wait_ge(S["gv_std"], c.next("gv_std"))
                V.reciprocal(small2[:, 8:10], small2[:, 4:6]).then_inc(S["dve_step"], c.one("dve_step"))
                dve.wait_ge(S["dve_step"], c.own("dve_step"))
                for tt in range(2):
                    last = TS(g2[:, tt, :], g2[:, tt, :], mv[:, tt * 2:tt * 2 + 1], small2[:, 8 + tt:9 + tt],
                              ALU.subtract, ALU.mult)
                last.then_inc(S["dve_step"], c.one("dve_step"))
                dve.wait_ge(S["dve_step"], c.own("dve_step"))
                two = lambda t: t.unsqueeze(1).to_broadcast([P, 2, T])
                dve.wait_ge(S["gmlp_in"], 16 * (l + 1))
                TT(g2, g2, two(gmw[:, 512:768]), ALU.mult).then_inc(S["dve_step"], c.one("dve_step"))
                dve.wait_ge(S["dve_step"], c.own("dve_step"))
                for g in range(4):
                    last = TT(gmw[:, g * P:(g + 1) * P], gmw[:, g * P:(g + 1) * P], t2("causal"), ALU.mult)
                TT(g2, g2, two(gmw[:, 768:1024]), ALU.add).then_inc(S["gv_ready"], c.one("gv_ready"))

            def layer_norm(gain, bias, l):
                dve.wait_ge(S["std_ready"], c.next("std_ready"))
                s = stdbuf()
                TT(hT3, hT3, s[:, 0:T].unsqueeze(1).to_broadcast([P, KT, T]), ALU.subtract).then_inc(S["std_taken"], c.one("std_taken"))
                dve.wait_ge(S["std_taken"], c.own("std_taken"))
                dve.wait_ge(S["std_ready"], c.next("std_ready"))
                s = stdbuf()
                V.reciprocal(rinv2[:, 0:T], s[:, 0:T]).then_inc(S["std_taken"], c.one("std_taken"))
                dve.wait_ge(S["std_taken"], c.own("std_taken"))
                for k in range(KT):
                    last = STT(U3[:, k, :], hT3[:, k, :], prm(gain, l, k), rinv2[:, 0:T], ALU.mult, ALU.mult)
                last.then_inc(S["dve_step"], c.one("dve_step"))
                dve.wait_ge(S["dve_step"], c.own("dve_step"))
                for k in range(KT):
                    last = TS(hT3[:, k, :], U3[:, k, :], prm(bias, l, k), None, ALU.add)
                last.then_inc(S["ln_done"], c.one("ln_done"))
                dve.wait_ge(S["ln_done"], c.own("ln_done"))

            def route():
                b = bank_in()
                lg = comb[:, 0:16]
                V.tensor_copy(lg, b[:, 0:16]).then_inc(S["top_logits"], c.one("top_logits"))
                dve.wait_ge(S["top_logits"], c.own("top_logits"))
                for tt in range(2):
                    last = V.max(comb[:, 16 + 8 * tt:24 + 8 * tt], lg[:, 8 * tt:8 * tt + 8])
                last.then_inc(S["dve_step"], c.one("dve_step"))
                dve.wait_ge(S["dve_step"], c.own("dve_step"))
                for tt in range(2):
                    V.max_index(ixb[:, 8 * tt:8 * tt + 8], comb[:, 16 + 8 * tt:24 + 8 * tt], lg[:, 8 * tt:8 * tt + 8])
                m = comb[:, 16:32].rearrange("p (s e) -> p s e", s=2)
                TT(comb[:, 34:36].unsqueeze(2), m[:, :, 1:2], m[:, :, 0:1], ALU.subtract).then_inc(S["top_arg"], c.one("top_arg"))
                dve.wait_ge(S["top_arg"], c.own("top_arg"))
                V.tensor_copy(comb[:, 48:64], ixb[:, :]).then_inc(S["dve_step"], c.one("dve_step"))
                dve.wait_ge(S["dve_step"], c.own("dve_step"))
                dve.wait_ge(S["top_exp"], c.next("top_exp"))
                TS(comb[:, 36:38], comb[:, 32:34], 1.0, None, ALU.add).then_inc(S["dve_step"], c.one("dve_step"))
                dve.wait_ge(S["dve_step"], c.own("dve_step"))
                V.reciprocal(comb[:, 38:40], comb[:, 36:38]).then_inc(S["dve_step"], c.one("dve_step"))
                dve.wait_ge(S["dve_step"], c.own("dve_step"))
                TT(comb[:, 40:42], comb[:, 32:34], comb[:, 38:40], ALU.mult).then_inc(S["dve_step"], c.one("dve_step"))
                dve.wait_ge(S["dve_step"], c.own("dve_step"))
                for tt in range(2):
                    TS(comb[:, 64 + 8 * tt:72 + 8 * tt], c1("iota"), comb[:, 48 + 8 * tt:49 + 8 * tt],
                       comb[:, 38 + tt:39 + tt], ALU.is_equal, ALU.mult)
                    last = TS(comb[:, 80 + 8 * tt:88 + 8 * tt], c1("iota"), comb[:, 49 + 8 * tt:50 + 8 * tt],
                              comb[:, 40 + tt:41 + tt], ALU.is_equal, ALU.mult)
                last.then_inc(S["dve_step"], c.one("dve_step"))
                dve.wait_ge(S["dve_step"], c.own("dve_step"))
                TT(lg, comb[:, 64:80], comb[:, 80:96], ALU.add).then_inc(S["comb_ready"], c.one("comb_ready"))
                V.tensor_copy(Y[0:8, 0:T], bank_in()[0:8, 0:T]).then_inc(S["ct_ready"], c.one("ct_ready"))
                for j in range(4):
                    V.tensor_copy(cbc[:, j * 512:(j + 1) * 512], bank_in()).then_inc(S["cbc_ready"], c.one("cbc_ready"))
                dve.wait_ge(S["cbc_ready"], c.own("cbc_ready"))

            for l in range(layers1):
                layer1(l)
            if layers2:
                if layers1:
                    dve.wait_ge(S["resid"], c.own("resid"))
                else:
                    dve.wait_ge(S["setup_done"], c.at("setup_done", 1))
                    dve.wait_ge(S["setup_in"], 48)
                dve.wait_ge(S["tab_in"], 16)
            for l in range(layers2):
                c.block = 1
                layer2(l)


def kernel(**inputs):
    import concourse.bacc as bacc
    from concourse.bass_utils import run_bass_kernel_spmd as run
    return _launch(inputs, LAYERS, LAYERS, bacc, run)


def _launch(inputs, layers1, layers2, bacc, run):
    plan = [x for l in range(layers1) for x in layer1_stream(l)] + \
           [x for l in range(layers2) for x in layer2_stream(l)]
    stream = np.zeros((len(plan), P, SLAB), np.float32)
    for n, (name, at, kind, first) in enumerate(plan):
        w = inputs[name][at]
        if kind == "cols":
            piece = w[:, first:first + WIDE]
            stream[n].reshape(P, KT, WIDE)[:, :, :piece.shape[1]] = piece.reshape(KT, P, -1).transpose(1, 0, 2)
        else:
            piece = w[first:first + 2 * P]
            for f in range(2):
                part = piece[f * P:(f + 1) * P]
                stream[n, :part.shape[0], f * D:(f + 1) * D] = part
    PAR, n_par = param_columns()
    params = np.zeros((P, n_par), np.float32)

    def put(name, l, v):
        params[:v.shape[0], PAR[name, l]:PAR[name, l] + v.shape[1]] = v

    def feat(v):
        return v.reshape(-1, P).T

    for l in range(LAYERS):
        for name in ("ffn1_norm", "mix_norm", "m_conv_b", "m_out_norm", "ffn2_norm", "ple_norm",
                     "b_norm_g_2", "ln1_g_2", "ln1_b_2", "ln2_g_2", "ln2_b_2", "m_conv_w", "conv_w_2"):
            put(name, l, feat(inputs[name][l].reshape(-1)))
        for name in ("a_q_norm", "a_k_norm"):
            put(name, l, np.concatenate([inputs[name][l]] * 2)[:, None])
        for name in ("m_igate_b", "m_fgate_b", "b_a_log_2", "b_dt_bias_2"):
            put(name, l, inputs[name][l][:, None])
        put("a_sinks", l, np.broadcast_to(inputs["a_sinks"][l][None], (P, Q_HEADS)))
        put("if_w", l, inputs["w_in"][l][:, I0:I0 + 8].reshape(KT, P, 8).transpose(1, 0, 2).reshape(P, 64))
        put("ba_w", l, inputs["w_in_2"][l][:, BETA1:BETA1 + 8].reshape(KT, P, 8).transpose(1, 0, 2).reshape(P, 64))
        put("a_bs_2", l, inputs["a_bs_2"][l].T)
    put("router", 0, inputs["moe_router_2"][0].reshape(KT, P, 8).transpose(1, 0, 2).reshape(P, 64))
    const, const2 = constants()
    gm = np.zeros((LAYERS, P, 512 + 512), np.float32)
    for l in range(LAYERS):
        gm[l, :, 0:512] = inputs["a_ws_2"][l].transpose(2, 0, 1).reshape(P, 512)
        gm[l, :, 512:768] = inputs["a_ln_g_2"][l][None]
        gm[l, :, 768:1024] = inputs["a_ln_b_2"][l][None]
    arrays = {
        "stream": stream,
        "x_t": np.ascontiguousarray(inputs["x"][0].T.reshape(KT, P, T).transpose(1, 0, 2)),
        "p_t": np.ascontiguousarray(inputs["p"][:, 0].transpose(0, 2, 1).reshape(LAYERS, 2, P, T).transpose(0, 2, 1, 3)),
        "params": params, "const": const, "const2": const2, "gmlp_w": gm,
    }
    nc = bacc.Bacc("TRN2", target_bir_lowering=False, num_devices=1)
    aps = [nc.dram_tensor(k, v.shape, F32, kind="ExternalInput").ap() for k, v in arrays.items()]
    out = nc.dram_tensor("out", (P, KT, T), F32, kind="ExternalOutput").ap()
    build(nc, *aps, out, layers1, layers2)
    r = run(nc, [arrays], core_ids=[0])
    return r.results[0]["out"].transpose(1, 0, 2).reshape(D, T).T.reshape(1, T, D)
```
